# Optimizing a Trainium2 kernel written in Bass

```python
import jax, jax.numpy as jnp
from jax import lax
import numpy as np
import math
import jax
import jax.numpy as jnp

D_MODEL = 1024
BATCH = 1
SEQ = 1024
DEPTH = 1

CHUNK = 64
N_MIXERS = 3
PLE_DIM = 256
EPS = 1e-6
MLA_HEADS = 16
MLA_Q_LORA = 384
MLA_KV_LORA = 256
MLA_NOPE = 64
MLA_ROPE = 32
MLA_V = 64
MLA_WIDTH = MLA_HEADS * MLA_V
MLA_IN = MLA_Q_LORA + MLA_KV_LORA + MLA_ROPE + MLA_WIDTH
ROPE_THETA = 10000.0
Q_BLOCK = 128
CONV_WIDTH = 3
CONV_DIM = D_MODEL
CONV_IN = 4 * CONV_DIM
MLSTM_HEADS = 4
MLSTM_INNER = 2 * D_MODEL
MLSTM_DV = MLSTM_INNER // MLSTM_HEADS
MLSTM_DK = MLSTM_DV // 2
MLSTM_IN = 2 * MLSTM_HEADS * MLSTM_DK + 3 * MLSTM_INNER + 2 * MLSTM_HEADS


def rmsnorm(x, g=None):
    xf = x.astype(jnp.float32)
    y = xf * lax.rsqrt(jnp.mean(xf * xf, axis=-1, keepdims=True) + EPS)
    if g is not None:
        y = y * g.astype(jnp.float32)
    return y.astype(x.dtype)

def rope_cos_sin(positions, dim, dtype):
    inv = ROPE_THETA ** (-jnp.arange(0, dim, 2, dtype=jnp.float32) / dim)
    ang = positions.astype(jnp.float32)[..., None] * inv
    return jnp.cos(ang).astype(dtype), jnp.sin(ang).astype(dtype)

def apply_rope(x, cos, sin):
    x1, x2 = jnp.split(x, 2, axis=-1)
    return jnp.concatenate([x1 * cos - x2 * sin, x1 * sin + x2 * cos], axis=-1)

def mla_mixer(h, cos, sin, w_in, q_norm, w_q_b, kv_norm, w_kv_b, w_out):
    B, S, _ = h.shape
    u = h @ w_in
    c_q, c_kv, k_rope, z = jnp.split(
        u, [MLA_Q_LORA, MLA_Q_LORA + MLA_KV_LORA, MLA_Q_LORA + MLA_KV_LORA + MLA_ROPE], axis=-1)
    q = (rmsnorm(c_q, q_norm) @ w_q_b).reshape(B, S, MLA_HEADS, MLA_NOPE + MLA_ROPE)
    q_nope = q[..., :MLA_NOPE]
    q_rope = apply_rope(q[..., MLA_NOPE:], cos[:, :, None], sin[:, :, None])
    kv = (rmsnorm(c_kv, kv_norm) @ w_kv_b).reshape(B, S, MLA_HEADS, MLA_NOPE + MLA_V)
    k_nope, v = kv[..., :MLA_NOPE], kv[..., MLA_NOPE:]
    k_rope = apply_rope(k_rope, cos, sin)
    scale = (MLA_NOPE + MLA_ROPE) ** -0.5
    outs = []
    for blk in range(S // Q_BLOCK):
        q0, q1 = blk * Q_BLOCK, (blk + 1) * Q_BLOCK
        s = (jnp.einsum('bqhd,bkhd->bhqk', q_nope[:, q0:q1], k_nope[:, :q1])
             + jnp.einsum('bqhd,bkd->bhqk', q_rope[:, q0:q1], k_rope[:, :q1])).astype(jnp.float32) * scale
        q_chunk = (q0 + jnp.arange(Q_BLOCK)) // CHUNK
        k_chunk = jnp.arange(q1) // CHUNK
        s = jnp.where(k_chunk[None, :] <= q_chunk[:, None], s, -jnp.inf)
        prob = jax.nn.softmax(s, axis=-1).astype(v.dtype)
        outs.append(jnp.einsum('bhqk,bkhd->bqhd', prob, v[:, :q1]))
    o = jnp.concatenate(outs, axis=1).reshape(B, S, MLA_WIDTH)
    return (o * jax.nn.silu(z)) @ w_out

def shortconv_mixer(h, w_in, conv_w, w_out):
    b_gate, c_gate, hx, z = jnp.split(h @ w_in, 4, axis=-1)
    y = lax.conv_general_dilated(
        c_gate * hx, conv_w[:, None, :].astype(hx.dtype), window_strides=(1,),
        padding=[(CONV_WIDTH - 1, 0)], dimension_numbers=('NWC', 'WIO', 'NWC'),
        feature_group_count=CONV_DIM)
    return (b_gate * y * jax.nn.silu(z)) @ w_out

def mlstm_chunk_step(carry, xs):
    C, n, m = carry
    q, k, v, ig, lf = xs
    L = q.shape[2]
    b = jnp.cumsum(lf, axis=-1)
    causal = jnp.tril(jnp.ones((L, L), dtype=bool))
    d_log = jnp.where(causal, b[..., :, None] - b[..., None, :] + ig[..., None, :], -jnp.inf)
    g = b + m[..., None]
    m_t = jnp.maximum(g, jnp.max(d_log, axis=-1))
    w_intra = jnp.exp(d_log - m_t[..., None])
    w_inter = jnp.exp(g - m_t)
    s = jnp.einsum('bhtd,bhsd->bhts', q, k) * w_intra
    num = (w_inter[..., None] * jnp.einsum('bhtd,bhdv->bhtv', q, C)
           + jnp.einsum('bhts,bhsv->bhtv', s, v))
    den = w_inter * jnp.einsum('bhtd,bhd->bht', q, n) + jnp.sum(s, axis=-1)
    h = num / jnp.maximum(jnp.abs(den), jnp.exp(-m_t))[..., None]
    b_last = b[..., -1]
    d_state = b_last[..., None] - b + ig
    m_new = jnp.maximum(b_last + m, jnp.max(d_state, axis=-1))
    w_s = jnp.exp(d_state - m_new[..., None])
    decay = jnp.exp(b_last + m - m_new)
    C = decay[..., None, None] * C + jnp.einsum('bhs,bhsd,bhsv->bhdv', w_s, k, v)
    n = decay[..., None] * n + jnp.einsum('bhs,bhsd->bhd', w_s, k)
    return (C, n, m_new), h

def mlstm_mixer(h, w_in, b_gates, w_out):
    B, S, _ = h.shape
    H, DK, DV = MLSTM_HEADS, MLSTM_DK, MLSTM_DV
    qk = H * DK
    u = h @ w_in
    q, k, v, o, z, gates = jnp.split(
        u, [qk, 2 * qk, 2 * qk + MLSTM_INNER, 2 * qk + 2 * MLSTM_INNER, 2 * qk + 3 * MLSTM_INNER], axis=-1)
    gates = gates.astype(jnp.float32) + b_gates.astype(jnp.float32)
    ig = gates[..., :H]
    lf = jax.nn.log_sigmoid(gates[..., H:])
    nc = S // CHUNK

    def to_chunks(t, d):
        return t.astype(jnp.float32).reshape(B, nc, CHUNK, H, d).transpose(1, 0, 3, 2, 4)

    def gate_chunks(t):
        return t.reshape(B, nc, CHUNK, H).transpose(1, 0, 3, 2)

    xs = (to_chunks(q, DK), to_chunks(k, DK) * (DK ** -0.5), to_chunks(v, DV),
          gate_chunks(ig), gate_chunks(lf))
    init = (jnp.zeros((B, H, DK, DV), jnp.float32), jnp.zeros((B, H, DK), jnp.float32),
            jnp.zeros((B, H), jnp.float32))
    _, hc = lax.scan(mlstm_chunk_step, init, xs)
    hs = hc.transpose(1, 0, 3, 2, 4).reshape(B, S, MLSTM_INNER).astype(h.dtype)
    return (jax.nn.sigmoid(o) * hs * jax.nn.silu(z)) @ w_out

def first_inputs(seed: int = 0) -> dict:
    key = jax.random.key(seed)
    ks = iter(jax.random.split(key, 32))
    n_mla = max(0, (DEPTH - 0 + 2) // 3)
    n_conv = max(0, (DEPTH - 1 + 2) // 3)
    n_mlstm = max(0, (DEPTH - 2 + 2) // 3)
    res_scale = (2.0 * DEPTH) ** -0.5

    def nrm(shape, scale):
        return jax.random.normal(next(ks), shape, jnp.float32) * scale

    def gain(shape):
        return 1.0 + nrm(shape, 0.02)

    x = nrm((BATCH, SEQ, D_MODEL), 1.0)
    p = nrm((DEPTH, BATCH, SEQ, PLE_DIM), 1.0)
    offsets = jax.random.randint(next(ks), (BATCH, 1), 0, 4096, dtype=jnp.int32)
    positions = (offsets + jnp.arange(SEQ, dtype=jnp.int32)[None, :]).astype(jnp.int32)
    norm_g = gain((DEPTH, D_MODEL))
    mla_w_in = nrm((n_mla, D_MODEL, MLA_IN), D_MODEL ** -0.5)
    mla_q_norm = gain((n_mla, MLA_Q_LORA))
    mla_w_q_b = nrm((n_mla, MLA_Q_LORA, MLA_HEADS * (MLA_NOPE + MLA_ROPE)), MLA_Q_LORA ** -0.5)
    mla_kv_norm = gain((n_mla, MLA_KV_LORA))
    mla_w_kv_b = nrm((n_mla, MLA_KV_LORA, MLA_HEADS * (MLA_NOPE + MLA_V)), MLA_KV_LORA ** -0.5)
    mla_w_out = nrm((n_mla, MLA_WIDTH, D_MODEL), MLA_WIDTH ** -0.5 * res_scale)
    conv_w_in = nrm((n_conv, D_MODEL, CONV_IN), D_MODEL ** -0.5)
    conv_w = nrm((n_conv, CONV_WIDTH, CONV_DIM), CONV_WIDTH ** -0.5)
    conv_w_out = nrm((n_conv, CONV_DIM, D_MODEL), CONV_DIM ** -0.5 * res_scale)
    mlstm_w_in = nrm((n_mlstm, D_MODEL, MLSTM_IN), D_MODEL ** -0.5)
    b_in = nrm((n_mlstm, MLSTM_HEADS), 0.1)
    b_f = jnp.linspace(3.0, 6.0, MLSTM_HEADS, dtype=jnp.float32)[None, :] + nrm((n_mlstm, MLSTM_HEADS), 0.1)
    mlstm_b_gates = jnp.concatenate([b_in, b_f], axis=-1)
    mlstm_w_out = nrm((n_mlstm, MLSTM_INNER, D_MODEL), MLSTM_INNER ** -0.5 * res_scale)
    ple_proj = nrm((DEPTH, PLE_DIM, D_MODEL), PLE_DIM ** -0.5 * res_scale)
    ple_gate = nrm((DEPTH, D_MODEL, D_MODEL), D_MODEL ** -0.5)
    final_norm = gain((D_MODEL,))
    return {"x": x, "p": p, "positions": positions, "norm_g": norm_g,
            "mla_w_in": mla_w_in, "mla_q_norm": mla_q_norm, "mla_w_q_b": mla_w_q_b,
            "mla_kv_norm": mla_kv_norm, "mla_w_kv_b": mla_w_kv_b, "mla_w_out": mla_w_out,
            "conv_w_in": conv_w_in, "conv_w": conv_w, "conv_w_out": conv_w_out,
            "mlstm_w_in": mlstm_w_in, "mlstm_b_gates": mlstm_b_gates, "mlstm_w_out": mlstm_w_out,
            "ple_proj": ple_proj, "ple_gate": ple_gate, "final_norm": final_norm}

def first_block(x, p, positions, norm_g, mla_w_in, mla_q_norm, mla_w_q_b, mla_kv_norm, mla_w_kv_b,
              mla_w_out, conv_w_in, conv_w, conv_w_out, mlstm_w_in, mlstm_b_gates, mlstm_w_out,
              ple_proj, ple_gate, final_norm):
    cos, sin = rope_cos_sin(positions, MLA_ROPE, x.dtype)
    for i in range(DEPTH):
        kind, j = i % N_MIXERS, i // N_MIXERS
        h = rmsnorm(x, norm_g[i])
        if kind == 0:
            y = mla_mixer(h, cos, sin, mla_w_in[j], mla_q_norm[j], mla_w_q_b[j],
                          mla_kv_norm[j], mla_w_kv_b[j], mla_w_out[j])
        elif kind == 1:
            y = shortconv_mixer(h, conv_w_in[j], conv_w[j], conv_w_out[j])
        else:
            y = mlstm_mixer(h, mlstm_w_in[j], mlstm_b_gates[j], mlstm_w_out[j])
        x = x + y
        gate = jax.nn.sigmoid(rmsnorm(x) @ ple_gate[i])
        x = x + gate * (p[i] @ ple_proj[i])
    return rmsnorm(x, final_norm)


A_DK = 128
A_DV = 128
A_HEADS = D_MODEL // (2 * A_DV)
CONV_K = 4
B_DK = 128
B_DV = 128
B_HEADS = D_MODEL // (2 * B_DV)
ROPE_BASE = 10000.0
N_GROUPS = 8
EXPERTS_PER_GROUP = 8
N_EXPERTS = N_GROUPS * EXPERTS_PER_GROUP
TOP_K = 2
D_EXPERT = 256

A_QK = A_HEADS * A_DK
A_V = A_HEADS * A_DV
A_CONV = 2 * A_QK + A_V
B_QK = B_HEADS * B_DK
B_V = B_HEADS * B_DV
D_MIX = A_V + B_V
IN_SIZES = (A_QK, A_QK, A_V, A_V, A_HEADS, A_HEADS, B_QK, B_QK, B_V, B_V)
D_IN = sum(IN_SIZES)


def rms_norm(x, w):
    xf = x.astype(jnp.float32)
    y = xf * lax.rsqrt(jnp.mean(xf * xf, axis=-1, keepdims=True) + EPS)
    return (y * w.astype(jnp.float32)).astype(x.dtype)

def l2norm(t):
    return t * lax.rsqrt(jnp.sum(t * t, axis=-1, keepdims=True) + EPS)

def to_heads(t, n_heads):
    b, s, _ = t.shape
    return t.reshape(b, s, n_heads, -1).transpose(0, 2, 1, 3)

def to_chunks(t):
    b, h, s = t.shape[:3]
    return t.reshape(b, h, s // CHUNK, CHUNK, *t.shape[3:])

def from_chunks(o):
    n, b, h, c, d = o.shape
    return jnp.moveaxis(o, 0, 2).reshape(b, h, n * c, d).transpose(0, 2, 1, 3)

def causal_conv(x, w):
    return lax.conv_general_dilated(
        x, w[:, None, :], window_strides=(1,), padding=[(CONV_K - 1, 0)],
        dimension_numbers=("NWC", "WIO", "NWC"), feature_group_count=x.shape[-1])

def rope(t, cos, sin):
    half = t.shape[-1] // 2
    t1, t2 = t[..., :half], t[..., half:]
    return jnp.concatenate([t1 * cos - t2 * sin, t1 * sin + t2 * cos], axis=-1)

def gated_delta_net(qkv, gate, beta_in, alpha_in, conv_w, a_log, dt_bias, norm_w):
    b, s, _ = qkv.shape
    qkv = jax.nn.silu(causal_conv(qkv, conv_w.astype(jnp.float32)))
    q, k, v = jnp.split(qkv, [A_QK, 2 * A_QK], axis=-1)
    q = l2norm(to_heads(q, A_HEADS)) * (A_DK ** -0.5)
    k = l2norm(to_heads(k, A_HEADS))
    v = to_heads(v, A_HEADS)
    beta = jax.nn.sigmoid(beta_in).transpose(0, 2, 1)
    g = (-jnp.exp(a_log.astype(jnp.float32))
         * jax.nn.softplus(alpha_in + dt_bias.astype(jnp.float32))).transpose(0, 2, 1)
    q, k, v, beta, g = (to_chunks(t) for t in (q, k, v, beta, g))
    gc = jnp.cumsum(g, axis=-1)
    causal = jnp.tril(jnp.ones((CHUNK, CHUNK), dtype=bool))
    strict = jnp.tril(jnp.ones((CHUNK, CHUNK), dtype=bool), -1)
    diff = gc[..., :, None] - gc[..., None, :]
    decay = jnp.where(causal, jnp.exp(jnp.where(causal, diff, 0.0)), 0.0)
    kb = k * beta[..., None]
    a_mat = jnp.where(strict, jnp.einsum("bhnid,bhnjd->bhnij", kb, k) * decay, 0.0)
    rhs = jnp.concatenate([v * beta[..., None], kb * jnp.exp(gc)[..., None]], axis=-1)
    uw = lax.linalg.triangular_solve(a_mat, rhs, left_side=True, lower=True, unit_diagonal=True)
    u, w = uw[..., :A_DV], uw[..., A_DV:]
    attn = jnp.einsum("bhnid,bhnjd->bhnij", q, k) * decay
    q_dec = q * jnp.exp(gc)[..., None]
    k_dec = k * jnp.exp(gc[..., -1:] - gc)[..., None]
    last = jnp.exp(gc[..., -1])

    def step(state, inp):
        q_c, k_c, u_c, w_c, attn_c, last_c = inp
        v_new = u_c - jnp.einsum("bhck,bhkv->bhcv", w_c, state)
        o_c = (jnp.einsum("bhck,bhkv->bhcv", q_c, state)
               + jnp.einsum("bhcj,bhjv->bhcv", attn_c, v_new))
        state = state * last_c[..., None, None] + jnp.einsum("bhck,bhcv->bhkv", k_c, v_new)
        return state, o_c

    xs = tuple(jnp.moveaxis(t, 2, 0) for t in (q_dec, k_dec, u, w, attn, last))
    s0 = jnp.zeros((b, A_HEADS, A_DK, A_DV), jnp.float32)
    _, o = lax.scan(step, s0, xs)
    o = from_chunks(o)
    o = rms_norm(o, norm_w) * jax.nn.silu(gate.reshape(b, s, A_HEADS, A_DV))
    return o.reshape(b, s, A_V)

def retention(q, k, v, gate, cos, sin, norm_w):
    b, s, _ = q.shape
    q = rope(to_heads(q, B_HEADS), cos, sin)
    k = rope(to_heads(k, B_HEADS), cos, sin) * (B_DK ** -0.5)
    v = to_heads(v, B_HEADS)
    log_gamma = jnp.log(1.0 - 2.0 ** (-5.0 - jnp.arange(B_HEADS, dtype=jnp.float32)))
    pos = jnp.arange(CHUNK, dtype=jnp.float32)
    rel = pos[:, None] - pos[None, :]
    decay = jnp.where(rel >= 0, jnp.exp(jnp.maximum(rel, 0.0) * log_gamma[:, None, None]), 0.0)
    q, k, v = (to_chunks(t) for t in (q, k, v))
    attn = jnp.einsum("bhnid,bhnjd->bhnij", q, k) * decay[None, :, None]
    inner = jnp.einsum("bhnij,bhnjv->bhniv", attn, v)
    q_dec = q * jnp.exp((pos + 1.0) * log_gamma[:, None])[None, :, None, :, None]
    k_dec = k * jnp.exp((CHUNK - 1.0 - pos) * log_gamma[:, None])[None, :, None, :, None]
    chunk_decay = jnp.exp(CHUNK * log_gamma)[None, :, None, None]

    def step(state, inp):
        q_c, k_c, v_c = inp
        o_c = jnp.einsum("bhck,bhkv->bhcv", q_c, state)
        state = state * chunk_decay + jnp.einsum("bhck,bhcv->bhkv", k_c, v_c)
        return state, o_c

    xs = tuple(jnp.moveaxis(t, 2, 0) for t in (q_dec, k_dec, v))
    s0 = jnp.zeros((b, B_HEADS, B_DK, B_DV), jnp.float32)
    _, cross = lax.scan(step, s0, xs)
    o = from_chunks(cross) + from_chunks(jnp.moveaxis(inner, 2, 0))
    o = rms_norm(o, norm_w.reshape(B_HEADS, B_DV)) * jax.nn.silu(gate.reshape(b, s, B_HEADS, B_DV))
    return o.reshape(b, s, B_V)

def hierarchical_moe(h, w_router_group, w_router_expert, w_gate, w_up, w_down):
    b, s, d = h.shape
    ht = h.reshape(b * s, d)
    hf = ht.astype(jnp.float32)
    g_logits = hf @ w_router_group.astype(jnp.float32)
    g_prob = jax.nn.softmax(g_logits, axis=-1)
    g_idx = jnp.argmax(g_logits, axis=-1)
    g_w = jnp.take_along_axis(g_prob, g_idx[:, None], axis=-1)[:, 0]
    e_logits = (hf @ w_router_expert.astype(jnp.float32)).reshape(-1, N_GROUPS, EXPERTS_PER_GROUP)
    e_logits = jnp.take_along_axis(e_logits, g_idx[:, None, None], axis=1)[:, 0]
    e_prob = jax.nn.softmax(e_logits, axis=-1)
    top_p, top_i = lax.top_k(e_prob, TOP_K)
    top_p = top_p / jnp.sum(top_p, axis=-1, keepdims=True)
    weights = (g_w[:, None] * top_p).reshape(-1)
    expert_id = (g_idx[:, None] * EXPERTS_PER_GROUP + top_i).reshape(-1).astype(jnp.int32)
    order = jnp.argsort(expert_id)
    tok = order // TOP_K
    xs = ht[tok]
    group_sizes = jnp.zeros((N_EXPERTS,), jnp.int32).at[expert_id].add(1)
    gate = lax.ragged_dot(xs, w_gate, group_sizes)
    up = lax.ragged_dot(xs, w_up, group_sizes)
    y = lax.ragged_dot((jax.nn.silu(gate) * up).astype(xs.dtype), w_down, group_sizes)
    y = y * weights[order].astype(y.dtype)[:, None]
    out = jnp.zeros_like(ht).at[tok].add(y)
    return out.reshape(b, s, d)

def second_inputs(seed: int = 0) -> dict:
    key = jax.random.key(seed)
    ks = jax.random.split(key, 20)
    f32 = jnp.float32

    def nrm(k, shape, scale):
        return jax.random.normal(k, shape, f32) * scale

    def gain(k, shape):
        return 1.0 + 0.02 * jax.random.normal(k, shape, f32)

    x = nrm(ks[0], (BATCH, SEQ, D_MODEL), 1.0)
    attn_norm = gain(ks[1], (DEPTH, D_MODEL))
    w_in = nrm(ks[2], (DEPTH, D_MODEL, D_IN), D_MODEL ** -0.5)
    conv_a = nrm(ks[3], (DEPTH, CONV_K, A_CONV), CONV_K ** -0.5)
    a_log = jnp.log(jax.random.uniform(ks[4], (DEPTH, A_HEADS), f32, 1.0, 16.0))
    dt = jnp.exp(jax.random.uniform(ks[5], (DEPTH, A_HEADS), f32, math.log(1e-3), math.log(1e-1)))
    dt_bias = dt + jnp.log(-jnp.expm1(-dt))
    norm_a = gain(ks[6], (DEPTH, A_DV))
    norm_b = gain(ks[7], (DEPTH, B_V))
    w_out = nrm(ks[8], (DEPTH, D_MIX, D_MODEL), D_MIX ** -0.5)
    ffn_norm = gain(ks[9], (DEPTH, D_MODEL))
    w_router_group = nrm(ks[10], (DEPTH, D_MODEL, N_GROUPS), D_MODEL ** -0.5)
    w_router_expert = nrm(ks[11], (DEPTH, D_MODEL, N_EXPERTS), D_MODEL ** -0.5)
    w_gate = nrm(ks[12], (DEPTH, N_EXPERTS, D_MODEL, D_EXPERT), D_MODEL ** -0.5)
    w_up = nrm(ks[13], (DEPTH, N_EXPERTS, D_MODEL, D_EXPERT), D_MODEL ** -0.5)
    w_down = nrm(ks[14], (DEPTH, N_EXPERTS, D_EXPERT, D_MODEL), D_EXPERT ** -0.5)
    final_norm = gain(ks[15], (D_MODEL,))
    return {"x": x, "attn_norm": attn_norm, "w_in": w_in, "conv_a": conv_a,
            "a_log": a_log, "dt_bias": dt_bias, "norm_a": norm_a, "norm_b": norm_b,
            "w_out": w_out, "ffn_norm": ffn_norm, "w_router_group": w_router_group,
            "w_router_expert": w_router_expert, "w_gate": w_gate, "w_up": w_up,
            "w_down": w_down, "final_norm": final_norm}

def second_block(x, attn_norm, w_in, conv_a, a_log, dt_bias, norm_a, norm_b, w_out, ffn_norm,
              w_router_group, w_router_expert, w_gate, w_up, w_down, final_norm):
    s = x.shape[1]
    pos = jnp.arange(s, dtype=jnp.float32)
    inv_freq = ROPE_BASE ** (-jnp.arange(0, B_DK, 2, dtype=jnp.float32) / B_DK)
    ang = pos[:, None] * inv_freq[None, :]
    cos, sin = jnp.cos(ang), jnp.sin(ang)
    offsets = [int(o) for o in np.cumsum(IN_SIZES)[:-1]]
    for l in range(DEPTH):
        h = rms_norm(x, attn_norm[l])
        proj = jnp.einsum("bsd,de->bse", h, w_in[l]).astype(jnp.float32)
        q_a, k_a, v_a, g_a, beta_a, alpha_a, q_b, k_b, v_b, g_b = jnp.split(proj, offsets, axis=-1)
        o_a = gated_delta_net(jnp.concatenate([q_a, k_a, v_a], axis=-1), g_a, beta_a, alpha_a,
                              conv_a[l], a_log[l], dt_bias[l], norm_a[l])
        o_b = retention(q_b, k_b, v_b, g_b, cos, sin, norm_b[l])
        mixed = jnp.concatenate([o_a, o_b], axis=-1).astype(x.dtype)
        x = x + jnp.einsum("bse,ed->bsd", mixed, w_out[l])
        h2 = rms_norm(x, ffn_norm[l])
        x = x + hierarchical_moe(h2, w_router_group[l], w_router_expert[l],
                                 w_gate[l], w_up[l], w_down[l])
    return rms_norm(x, final_norm)


def setup_inputs(seed=0):
    out = dict(first_inputs(seed))
    for name, value in second_inputs(seed + 1).items():
        if name != "x":
            out[name + "_2"] = value
    return out


def reference(
    x, p, positions, norm_g, mla_w_in, mla_q_norm, mla_w_q_b, mla_kv_norm, mla_w_kv_b,
    mla_w_out, conv_w_in, conv_w, conv_w_out, mlstm_w_in, mlstm_b_gates, mlstm_w_out, ple_proj,
    ple_gate, final_norm, attn_norm_2, w_in_2, conv_a_2, a_log_2, dt_bias_2, norm_a_2, norm_b_2,
    w_out_2, ffn_norm_2, w_router_group_2, w_router_expert_2, w_gate_2, w_up_2, w_down_2,
    final_norm_2,
):
    x = first_block(
        x, p, positions, norm_g, mla_w_in, mla_q_norm, mla_w_q_b, mla_kv_norm, mla_w_kv_b,
        mla_w_out, conv_w_in, conv_w, conv_w_out, mlstm_w_in, mlstm_b_gates, mlstm_w_out,
        ple_proj, ple_gate, final_norm,
    )
    return second_block(
        x, attn_norm_2, w_in_2, conv_a_2, a_log_2, dt_bias_2, norm_a_2, norm_b_2, w_out_2,
        ffn_norm_2, w_router_group_2, w_router_expert_2, w_gate_2, w_up_2, w_down_2,
        final_norm_2,
    )


_drawn_inputs = setup_inputs


def setup_inputs(seed=0):
    import zlib

    import numpy as np

    out = dict(_drawn_inputs(seed))
    spreads = {}
    factors = {'norm_g': 6.865,
     'mla_q_norm': 8.0,
     'mla_kv_norm': 8.0,
     'norm_a_2': 3.854,
     'norm_b_2': 4.569,
     'ffn_norm_2': 2.705,
     'final_norm_2': 2.879}
    for name, (base, spread) in spreads.items():
        noise = np.random.default_rng([zlib.crc32(name.encode()), seed]).standard_normal(out[name].shape)
        drawn = base * np.exp(spread * noise) if base else spread * noise
        out[name] = jnp.asarray(drawn.astype(out[name].dtype))
    for name, factor in factors.items():
        out[name] = (out[name] * factor).astype(out[name].dtype)
    return out
```

```python
import numpy as np
from contextlib import ExitStack

import concourse.bass as bass
from concourse import mybir

F32 = mybir.dt.float32
I32 = mybir.dt.int32
F32R = mybir.dt.float32r
ALU = mybir.AluOpType
ACT = mybir.ActivationFunctionType
AX = mybir.AxisListType

P = 128
D = 1024
S = 1024
T = S // P
KD = D // P
HEADS, NOPE, ROPE, VD = 16, 64, 32, 64
QK = NOPE + ROPE
LQ, LKV = 384, 256
U_IN = LQ + LKV + ROPE + HEADS * VD
PLE = 256
EPS = 1e-6
BANK = 512

AH, BH, HD = 4, 4, 128
CONV_CH, TAPS = 3 * AH * HD, 4
EXPERTS, GROUPS, PER_GROUP, DE = 64, 8, 8, 256
N_BLOCKS = 2 * S // P + EXPERTS - 1
NOWHERE = 4096.0

CONST = {}
_at = 0
for _name, _n in (("ident", P), ("tri", P), ("ones", P), ("inv", ROPE // 2), ("levels", 7 * P), ("decay", BH * P),
                  ("qdec", BH), ("kdec", BH), ("gend", BH), ("iota", P), ("neghalf", 8), ("before", P), ("asg", 2 * T), ("pcol", 1)):
    CONST[_name] = (_at, _n)
    _at += _n
N_CONST = _at
GAMMA_END = [float((1.0 - 2.0 ** (-5.0 - h)) ** P) for h in range(BH)]


def constants():
    c = np.zeros((P, N_CONST), np.float64)
    i, j = np.arange(P)[:, None], np.arange(P)[None, :]

    def put(name, x):
        at, n = CONST[name]
        c[:, at:at + n] = x

    put("ident", i == j)
    put("tri", i <= j)
    put("ones", 1.0)
    put("inv", 10000.0 ** (-np.arange(0, ROPE, 2) / ROPE)[None, :])
    put("levels", np.concatenate([((i >> s) % 2 == 1) & ((j >> s) == (i >> s) - 1) for s in range(7)], axis=1))
    lg = np.log(1.0 - 2.0 ** (-5.0 - np.arange(BH)))
    put("decay", np.concatenate([np.where(i <= j, np.exp(np.maximum(j - i, 0) * lg[h]) * HD ** -0.5, 0.0) for h in range(BH)], axis=1))
    put("qdec", np.exp((np.arange(P)[:, None] + 1.0) * lg[None, :]))
    put("kdec", np.exp((P - 1.0 - np.arange(P)[:, None]) * lg[None, :]) * HD ** -0.5)
    put("gend", np.exp(P * lg)[None, :])
    put("iota", j)
    put("neghalf", -0.5)
    put("before", i < j)
    put("asg", np.concatenate([2 * (np.arange(T)[None, :] * P + i) + k for k in range(2)], axis=1) - NOWHERE)
    put("pcol", i)
    ang = np.arange(S, dtype=np.float32)[:, None] * (10000.0 ** (-np.arange(0, HD, 2) / HD)).astype(np.float32)[None, :]
    cs = np.concatenate([np.cos(ang.astype(np.float64)), np.sin(ang.astype(np.float64))], axis=1)
    return c.astype(np.float32), cs.astype(np.float32)


class Jobs:

    def __init__(self, base, banks, steps):
        self.banks, self.base = list(banks), dict((b, base[b]) for b in set(banks))
        for b in set(banks):
            base[b] += self.banks.count(b) * steps

    def before(self, j, t):
        b = self.banks[j]
        return t * self.banks.count(b) + (self.base[b] + self.banks[:j].count(b))


def build(nc, A, out):
    ctx = ExitStack()
    with ctx:
        def sem(name):
            return ctx.enter_context(nc.semaphore(name))

        base_off = 16512

        def sb(name, shape, off, dt=F32):
            return nc.alloc_sbuf_tensor_at(name, shape, dt, offset=base_off + off)

        def dram(name, shape, dt=F32):
            return nc.dram_tensor(name, shape, dt, kind="Internal").ap()

        s_const = sem("const_in")

        s_alone = sem("register_waits")

        def wait(eng, semaphore, value):
            if not isinstance(value, int):
                eng.wait_ge(semaphore, value)
                if eng.engine in (mybir.EngineType.Pool, mybir.EngineType.SP):
                    eng.sem_inc(s_alone, 1)
            elif value > 0:
                eng.wait_ge(semaphore, value)

        ps = ctx.enter_context(nc.psum_tensor("ps", [P, 8, BANK], F32))
        bank_full = [sem(f"bank_full{b}") for b in range(8)]
        bank_free = [sem(f"bank_free{b}") for b in range(8)]
        base = [0] * 8

        def job_start(pe, jobs, j, t):
            b = jobs.banks[j]
            wait(pe, bank_free[b], jobs.before(j, t))
            return ps[:, b, :]

        def job_end(mm, jobs, j):
            mm.then_inc(bank_full[jobs.banks[j]], 1)

        def job_read(eng, jobs, j, t):
            b = jobs.banks[j]
            wait(eng, bank_full[b], jobs.before(j, t) + 1)
            return ps[:, b, :]

        def job_done(ins, jobs, j):
            ins.then_inc(bank_free[jobs.banks[j]], 1)

        def job_copied(pe, jobs, j, t):
            wait(pe, bank_free[jobs.banks[j]], jobs.before(j, t) + 1)

        def bc(ap, n):
            return ap.unsqueeze(2).to_broadcast([ap.shape[0], ap.shape[1], n])

        def bc1(ap, n):
            return ap.unsqueeze(1).to_broadcast([ap.shape[0], n, ap.shape[1]])

        KB = 1024
        consts = sb("consts", [P, N_CONST], 0)
        small0 = (N_CONST * 4 + 31) // 32 * 32

        def const(name):
            at, n = CONST[name]
            return consts[:, at:at + n]

        ident = const("ident")
        ones = const("ones")
        tri = const("tri")
        neghalf = const("neghalf")
        ROWS = {"norm_g": (0, 8), "q_norm": (8, 3), "kv_norm": (11, 2), "attn_norm": (13, 8), "ffn_norm": (21, 8),
                "conv": (29, 48)}
        NR = 77
        o = small0
        gain_rows = sb("gain_rows", [NR, P], o); o += 512
        gain_cols = sb("gain_cols", [P, NR], o); o += 320

        def gain(name):
            at, n = ROWS[name]
            return gain_cols[:, at:at + n]

        pos_i = sb("pos_i", [P, T], o, I32); o += 32
        pos_f = sb("pos_f", [P, T], o); o += 32
        cos = sb("cos", [P, T, ROPE // 2], o); o += 512
        sin = sb("sin", [P, T, ROPE // 2], o); o += 512
        ang = sb("ang", [P, T, ROPE // 2], o); o += 512
        turns = sb("turns", [P, T, ROPE // 2], o); o += 512
        stats = sb("stats", [P, 128], o); o += 512
        ba = sb("ba", [P, T, 2 * AH], o); o += 256
        o = (o + 1023) // 1024 * 1024
        base0 = o

        s_phase = sem("phases_done")
        PH_A, PH_B, PH_C, PH_D, PH_M = 1, 2, 3, 4, 5
        s_small = sem("small_in")
        s_cols = sem("gain_cols_ready")
        s_rope = sem("rope_ready")
        s_ropec = sem("rope_chain")

        o = base0
        v_all = sb("v_all", [P, T, HEADS * VD], o); o += 32 * KB
        o_a = o
        w_u = sb("w_u", [P, KD, U_IN], o); o += KD * U_IN * 4
        w_q = sb("w_q", [P, 3, HEADS * QK], o); o += 3 * HEADS * QK * 4
        w_kv = sb("w_kv", [P, 2, HEADS * (NOPE + VD)], o); o += 2 * HEADS * (NOPE + VD) * 4
        x_in = [sb(f"x_in{p}", [P, D], o + 4 * KB * p) for p in range(2)]; o += 8 * KB
        x_t = [sb(f"x_t{p}", [P, KD, P], o + 4 * KB * p) for p in range(2)]; o += 8 * KB
        junk_a = sb("junk_a", [P, D], o); o += 4 * KB
        lat = [sb(f"lat{p}", [P, LQ + LKV], o + 2560 * p) for p in range(2)]; o += 5 * KB
        lat_t = sb("lat_t", [P, 5, P], o); o += 2560
        q_tok = sb("q_tok", [P, HEADS + 1, QK], o); o += 17 * QK * 4
        k_tok = sb("k_tok", [P, HEADS, QK], o); o += 16 * QK * 4
        rot_c = sb("rot_c", [P, HEADS + 1, ROPE], o); o += 17 * ROPE * 4
        rot_s = sb("rot_s", [P, HEADS + 1, ROPE], o); o += 17 * ROPE * 4
        q_feat = sb("q_feat", [QK, HEADS, P], o); o += 8 * KB
        sz_out = [sb(f"sz_out{p}", [P, HEADS * VD], o + 4 * KB * p) for p in range(2)]; o += 8 * KB
        k_feat = sb("k_feat", [QK, HEADS, P], o); o += 8 * KB
        assert base_off + o <= 229344, o
        q_d = dram("q_d", (HEADS, QK, S))
        k_d = dram("k_d", (HEADS, QK, S))
        sz_d = dram("sz_d", (S, HEADS * VD))

        A_X, A_U, A_C, A_Q, A_KV, A_QT, A_KT = 0, 2, 6, 8, 12, 16, 20
        a_jobs = Jobs(base, [0, 1, 2, 3, 0, 1] + [4, 5, 6, 7] * 4 + [4, 5], T)
        s_wu = [sem(f"w_u_in{g}") for g in range(4)]; s_wqkv = sem("w_qkv_in")
        s_xin = [sem(f"x_in_in{p}") for p in range(2)]
        s_xsq = sem("x_squared")
        s_xrs = sem("x_rstd")
        s_lat = sem("latents_copied")
        s_lsq = sem("latents_squared")
        s_lrs = sem("latent_rstd")
        s_qtok = sem("q_tok_copied")
        s_rot = sem("rotated")
        s_ktok = sem("k_tok_ready")
        s_qst = sem("q_stored"); s_kst = sem("k_stored")
        s_qf = sem("q_feat_copied"); s_kf = sem("k_feat_copied")
        s_sz = [sem(f"silu_z_ready{p}") for p in range(2)]
        s_szst = [sem(f"silu_z_stored{p}") for p in range(2)]

        ss_x = [stats[:, 0 + p:1 + p] for p in range(2)]
        rs_x = [stats[:, 2 + p:3 + p] for p in range(2)]
        ms_x = stats[:, 4:5]
        ss_l = [stats[:, 6 + 2 * p:8 + 2 * p] for p in range(2)]
        ms_l = stats[:, 10:12]
        rs_l = [stats[:, 12 + 2 * p:14 + 2 * p] for p in range(2)]
        rs_lq = stats[:, 16:17]

        def setup_sp(sp):
            sp.dma_start(consts[:, :], A["c_table"]).then_inc(s_const, 16)
            sp.dma_start(x_in[0][:, :], A["x"][0, 0:P, :]).then_inc(s_xin[0], 16)
            at = ROWS["norm_g"][0]
            sp.dma_start(gain_rows[at:at + 8, :], A["norm_g"].rearrange("a (k p) -> (a k) p", p=P)).then_inc(s_small, 16)
            at = ROWS["q_norm"][0]
            sp.dma_start(gain_rows[at:at + 3, :], A["mla_q_norm"].rearrange("a (k p) -> (a k) p", p=P)).then_inc(s_small, 16)
            at = ROWS["kv_norm"][0]
            sp.dma_start(gain_rows[at:at + 2, :], A["mla_kv_norm"].rearrange("a (k p) -> (a k) p", p=P)).then_inc(s_small, 16)
            at = ROWS["attn_norm"][0]
            sp.dma_start(gain_rows[at:at + 8, :], A["attn_norm_2"].rearrange("a (k p) -> (a k) p", p=P)).then_inc(s_small, 16)
            at = ROWS["ffn_norm"][0]
            sp.dma_start(gain_rows[at:at + 8, :], A["ffn_norm_2"].rearrange("a (k p) -> (a k) p", p=P)).then_inc(s_small, 16)
            at = ROWS["conv"][0]
            sp.dma_start(gain_rows[at:at + 48, :], A["conv_a_2"].rearrange("a k (c p) -> (a k c) p", p=P)).then_inc(s_small, 16)
            sp.dma_start(pos_i[:, :], A["positions"].rearrange("a (t p) -> p (a t)", p=P), allow_slow_non_contiguous=True).then_inc(s_small, 16)
            wu = A["mla_w_in"][0].rearrange("(k p) n -> p k n", p=P)
            for g, (c0, cn) in enumerate(U_COLS):
                sp.dma_start(w_u[:, :, c0:c0 + cn], wu[:, :, c0:c0 + cn]).then_inc(s_wu[g], 16)
            sp.dma_start(w_q[:, :, :], A["mla_w_q_b"][0].rearrange("(k p) n -> p k n", p=P)).then_inc(s_wqkv, 16)
            sp.dma_start(w_kv[:, :, :], A["mla_w_kv_b"][0].rearrange("(k p) n -> p k n", p=P)).then_inc(s_wqkv, 16)

        def setup_pe(pe):
            pe.wait_ge(s_const, 16)
            pe.wait_ge(s_small, 7 * 16)
            pe.transpose(ps[:, 7, 0:NR], gain_rows[:, :], ident[0:NR, 0:NR]).then_inc(s_cols, 1)

        def setup_dve(v):
            v.wait_ge(s_cols, 1)
            v.tensor_copy(gain_cols[:, :], ps[:, 7, 0:NR]).then_inc(s_cols, 1)
            n = 0

            def link(ins):
                nonlocal n
                n += 1
                ins.then_inc(s_ropec, 1)
                v.wait_ge(s_ropec, n)

            magic = 1.5 * 2.0 ** 23
            c1 = 6.28125
            c2 = float(np.array([np.float32(2 * np.pi - 6.28125).view(np.int32) & -8192], np.int32).view(np.float32)[0])
            c3 = float(np.float32(2 * np.pi - c1 - c2))
            v.wait_ge(s_small, 7 * 16)
            link(v.tensor_copy(pos_f[:, :], pos_i[:, :]))
            link(v.tensor_tensor(ang[:, :, :], bc(pos_f[:, :], ROPE // 2), bc1(const("inv"), T), ALU.mult))
            for table, shift in ((sin, 0.0), (cos, 0.25)):
                link(v.tensor_scalar(turns[:, :, :], ang[:, :, :], 1.0 / (2 * np.pi), shift, ALU.mult, ALU.add))
                link(v.tensor_scalar(turns[:, :, :], turns[:, :, :], magic, magic, ALU.add, ALU.subtract))
                link(v.scalar_tensor_tensor(table[:, :, :], turns[:, :, :], -c1, ang[:, :, :], ALU.mult, ALU.add))
                link(v.scalar_tensor_tensor(table[:, :, :], turns[:, :, :], -c2, table[:, :, :], ALU.mult, ALU.add))
                link(v.scalar_tensor_tensor(table[:, :, :], turns[:, :, :], -c3, table[:, :, :], ALU.mult, ALU.add))
                if shift:
                    link(v.tensor_scalar(table[:, :, :], table[:, :, :], np.pi / 2, None, ALU.add))
                link(v.tensor_scalar(table[:, :, :], table[:, :, :], 3.1415925, -3.1415925, ALU.min, ALU.max))
            v.tensor_scalar(table[:, :, :], table[:, :, :], 1.0, None, ALU.mult).then_inc(s_rope, 1)

        def setup_act(act):
            act.wait_ge(s_rope, 1)
            act.activation(sin[:, :, :], sin[:, :, :], ACT.Sin).then_inc(s_rope, 1)
            act.activation(cos[:, :, :], cos[:, :, :], ACT.Sin).then_inc(s_rope, 1)

        def two_stage(eng, step, tiles=T):
            step((0, 0, 0), None)
            with eng.Fori(0, (tiles - 2) // 2) as i:
                step((2 * i + 1, i, 1), (2 * i, i, 0))
                step((2 * i + 2, i + 1, 0), (2 * i + 1, i, 1))
            m = tiles // 2 - 1
            step((2 * m + 1, m, 1), (2 * m, m, 0))
            step(None, (2 * m + 1, m, 1))

        def three_stage(eng, step, tiles=T):
            step((0, 0, 0), None, None)
            step((1, 0, 1), (0, 0, 0), None)
            with eng.Fori(0, (tiles - 2) // 2) as i:
                step((2 * i + 2, i + 1, 0), (2 * i + 1, i, 1), (2 * i, i, 0))
                step((2 * i + 3, i + 1, 1), (2 * i + 2, i + 1, 0), (2 * i + 1, i, 1))
            m = tiles // 2 - 1
            step(None, (2 * m + 1, m, 1), (2 * m, m, 0))
            step(None, None, (2 * m + 1, m, 1))

        U_COLS = [(0, LQ), (LQ, LKV + ROPE), (LQ + LKV + ROPE, 512), (LQ + LKV + ROPE + 512, 512)]

        def a_sp(sp):
            def step(new, old):
                if new:
                    t, m, p = new
                    if not isinstance(t, int) or t > 0:
                        wait(sp, s_xsq, t - 1)
                        wait(sp, bank_full[1], (t - 1) * 2)
                        sp.dma_start(x_in[p][:, :], A["x"].rearrange("a (t p) n -> p (a t) n", p=P)[:, bass.ds(t, 1), :]
                                     .rearrange("p a n -> p (a n)")).then_inc(s_xin[p], 16)
            two_stage(sp, step)

        def a_pe(pe):
            def step(new, old):
                if new:
                    t, m, p = new
                    wait(pe, s_xin[p], m * 16 + 16)
                    for j in range(2):
                        b = job_start(pe, a_jobs, A_X + j, t)
                        for k in range(4):
                            mm = pe.transpose(b[:, k * P:(k + 1) * P], x_in[p][:, (4 * j + k) * P:(4 * j + k + 1) * P], ident)
                        job_end(mm, a_jobs, A_X + j)
                if old:
                    t, m, p = old
                    pe.wait_ge(s_lat, 2 * t + 2)
                    for j, (k0, kn) in enumerate(((0, 3), (3, 2))):
                        b = job_start(pe, a_jobs, A_C + j, t)
                        for k in range(kn):
                            mm = pe.transpose(b[:, k * P:(k + 1) * P], lat[p][:, (k0 + k) * P:(k0 + k + 1) * P], ident)
                        job_end(mm, a_jobs, A_C + j)
                    if isinstance(t, int) and t == 0:
                        pe.wait_ge(s_wqkv, 32)
                    for j0, k0, kn, w, width in ((A_Q, 0, 3, w_q, 4 * QK), (A_KV, 3, 2, w_kv, 4 * (NOPE + VD))):
                        job_copied(pe, a_jobs, A_C + k0 // 3, t)
                        for g in range(4):
                            b = job_start(pe, a_jobs, j0 + g, t)
                            for k in range(kn):
                                mm = pe.matmul(b[:, 0:width], lat_t[:, k0 + k, :], w[:, k, g * width:(g + 1) * width],
                                               start=(k == 0), stop=(k == kn - 1))
                            job_end(mm, a_jobs, j0 + g)
                if new:
                    t, m, p = new
                    for j in range(2):
                        job_copied(pe, a_jobs, A_X + j, t)
                    for g, (c0, cn) in enumerate(U_COLS):
                        if isinstance(t, int) and t == 0:
                            pe.wait_ge(s_wu[g], 16)
                        b = job_start(pe, a_jobs, A_U + g, t)
                        for k in range(KD):
                            mm = pe.matmul(b[:, 0:cn], x_t[p][:, k, :], w_u[:, k, c0:c0 + cn], start=(k == 0), stop=(k == KD - 1))
                        job_end(mm, a_jobs, A_U + g)
                if old:
                    t, m, p = old
                    pe.wait_ge(s_rot, 4 * t + 4)
                    for j0, src, ready in ((A_QT, q_tok, None), (A_KT, k_tok, s_ktok)):
                        if ready is not None:
                            pe.wait_ge(s_ktok, t + 1)
                        for g in range(4):
                            b = job_start(pe, a_jobs, j0 + g, t)
                            for h in range(4):
                                mm = pe.transpose(b[0:QK, h * P:(h + 1) * P], src[:, 4 * g + h, :], ident)
                            job_end(mm, a_jobs, j0 + g)
            two_stage(pe, step)

        def a_act(act):
            def step(new, old):
                if new:
                    t, m, p = new
                    act.wait_ge(s_xin[p], m * 16 + 16)
                    act.activation(junk_a[:, :], x_in[p][:, :], ACT.Square, accum_out=ss_x[p]).then_inc(s_xsq, 1)
                if old:
                    t, m, p = old
                    act.wait_ge(s_lrs, 3 * t + 3)
                    for g in range(4):
                        b = job_read(act, a_jobs, A_Q + g, t)
                        ins = act.activation(q_tok[:, 4 * g:4 * g + 4, :].rearrange("p h n -> p (h n)"), b[:, 0:4 * QK],
                                             ACT.Copy, scale=rs_lq)
                        job_done(ins, a_jobs, A_Q + g)
                    for g in range(4):
                        b = job_read(act, a_jobs, A_KV + g, t)
                        bv = b.rearrange("p (h n) -> p h n", h=4)
                        act.activation(k_tok[:, 4 * g:4 * g + 4, 0:NOPE], bv[:, :, 0:NOPE], ACT.Copy, scale=rs_l[p][:, 1:2])
                        ins = act.activation(v_all[:, bass.ds(t, 1), 256 * g:256 * g + 256].rearrange("p a (h n) -> p (a h) n", h=4),
                                             bv[:, :, NOPE:], ACT.Copy, scale=rs_l[p][:, 1:2])
                        job_done(ins, a_jobs, A_KV + g)
                if new:
                    t, m, p = new
                    act.wait_ge(s_xrs, 2 * t + 2)
                    b = job_read(act, a_jobs, A_U + 0, t)
                    job_done(act.activation(lat[p][:, 0:LQ], b[:, 0:LQ], ACT.Copy, scale=rs_x[p]), a_jobs, A_U + 0)
                    b = job_read(act, a_jobs, A_U + 1, t)
                    act.activation(lat[p][:, LQ:LQ + LKV], b[:, 0:LKV], ACT.Copy, scale=rs_x[p]).then_inc(s_lat, 2)
                    job_done(act.activation(krope[p][:, :], b[:, LKV:LKV + ROPE], ACT.Copy, scale=rs_x[p]), a_jobs, A_U + 1)
                    wait(act, s_szst[p], 16 * m)
                    for g in range(2):
                        b = job_read(act, a_jobs, A_U + 2 + g, t)
                        job_done(act.activation(sz_out[p][:, 512 * g:512 * g + 512], b, ACT.Silu, scale=rs_x[p]),
                                 a_jobs, A_U + 2 + g)
                if old:
                    t, m, p = old
                    wait(act, s_kst, 16 * t)
                    for g in range(4):
                        b = job_read(act, a_jobs, A_KT + g, t)
                        ins = act.activation(k_feat[:, 4 * g:4 * g + 4, :].rearrange("p h n -> p (h n)"), b[0:QK, :], ACT.Copy)
                        job_done(ins, a_jobs, A_KT + g)
            two_stage(act, step)

        krope = [sb(f"krope{p}", [P, ROPE], o + 128 * p) for p in range(2)]; o += 256
        assert base_off + o <= 229344, o

        def a_dve(v):
            def step(new, old):
                if new:
                    t, m, p = new
                    if isinstance(t, int) and t == 0:
                        v.wait_ge(s_cols, 2)
                    for j in range(2):
                        b = job_read(v, a_jobs, A_X + j, t)
                        ins = v.tensor_tensor(x_t[p][:, 4 * j:4 * j + 4, :], b.rearrange("p (k n) -> p k n", k=4),
                                              bc(gain("norm_g")[:, 4 * j:4 * j + 4], P), ALU.mult)
                        job_done(ins, a_jobs, A_X + j)
                if old:
                    t, m, p = old
                    for j, (k0, kn) in enumerate(((0, 3), (3, 2))):
                        b = job_read(v, a_jobs, A_C + j, t)
                        ins = v.tensor_tensor(lat_t[:, k0:k0 + kn, :], b[:, 0:kn * P].rearrange("p (k n) -> p k n", k=kn),
                                              bc(gain("q_norm" if j == 0 else "kv_norm"), P), ALU.mult)
                        job_done(ins, a_jobs, A_C + j)
                if new:
                    t, m, p = new
                    v.wait_ge(s_lat, 2 * t + 2)
                    v.tensor_tensor_reduce(junk_l[:, 0:LQ], lat[p][:, 0:LQ], lat[p][:, 0:LQ], 1.0 / LQ, 0.0, ALU.mult, ALU.add,
                                           ss_l[p][:, 0:1]).then_inc(s_lsq, 1)
                    v.tensor_tensor_reduce(junk_l[:, LQ:LQ + LKV], lat[p][:, LQ:LQ + LKV], lat[p][:, LQ:LQ + LKV], 1.0 / LKV, 0.0,
                                           ALU.mult, ALU.add, ss_l[p][:, 1:2]).then_inc(s_lsq, 1)
                if old:
                    t, m, p = old
                    wait(v, s_qst, 16 * t)
                    for g in range(4):
                        b = job_read(v, a_jobs, A_QT + g, t)
                        ins = v.tensor_copy(q_feat[:, 4 * g:4 * g + 4, :].rearrange("p h n -> p (h n)"), b[0:QK, :])
                        job_done(ins, a_jobs, A_QT + g)
            two_stage(v, step)

        junk_l = sb("junk_l", [P, LQ + LKV], o); o += 2560
        assert base_off + o <= 229344, o

        def rstd(pool, out_, ms, ss, n, chain, count, scale=1.0):
            pool.tensor_scalar(ms, ss, scale, EPS, ALU.mult, ALU.add).then_inc(chain, 1)
            wait(pool, chain, count + 1)
            pool.tensor_tensor(out_, ms, neghalf[:, 0:n], ALU.pow).then_inc(chain, 1)

        def a_pool(pool):
            def step(new, old):
                if new:
                    t, m, p = new
                    wait(pool, s_xsq, t + 1)
                    rstd(pool, rs_x[p], ms_x, ss_x[p], 1, s_xrs, 2 * t, 1.0 / D)
                if old:
                    t, m, p = old
                    if isinstance(t, int) and t == 0:
                        wait(pool, s_rope, 3)
                    wait(pool, s_lsq, 2 * t + 2)
                    rstd(pool, rs_l[p], ms_l, ss_l[p], 2, s_lrs, 3 * t)
                    wait(pool, s_lrs, 3 * t + 2)
                    pool.tensor_scalar(rs_lq, rs_l[p][:, 0:1], QK ** -0.5, None, ALU.mult).then_inc(s_lrs, 1)
                    for g in range(4):
                        wait(pool, bank_free[a_jobs.banks[A_Q + g]], a_jobs.before(A_Q + g, t) + 1)
                    pool.tensor_copy(q_tok[:, HEADS, NOPE:], krope[p][:, :]).then_inc(s_krc, 1)
                    wait(pool, s_krc, t + 1)
                    x = q_tok[:, :, NOPE:]
                    half = ROPE // 2
                    for d_, table in ((rot_c, cos), (rot_s, sin)):
                        cs = table[:, bass.ds(t, 1), :]
                        for e in range(2):
                            ins = pool.tensor_tensor(d_[:, :, e * half:(e + 1) * half], x[:, :, e * half:(e + 1) * half],
                                                     cs.to_broadcast([P, HEADS + 1, half]), ALU.mult)
                        ins.then_inc(s_rot, 1)
                    wait(pool, s_rot, 4 * t + 2)
                    pool.tensor_tensor(x[:, :, 0:half], rot_c[:, :, 0:half], rot_s[:, :, half:], ALU.subtract).then_inc(s_rot, 1)
                    pool.tensor_tensor(x[:, :, half:], rot_c[:, :, half:], rot_s[:, :, 0:half], ALU.add).then_inc(s_rot, 1)
                    wait(pool, s_rot, 4 * t + 4)
                    pool.tensor_copy(k_tok[:, :, NOPE:], q_tok[:, HEADS:HEADS + 1, NOPE:].to_broadcast([P, HEADS, ROPE])).then_inc(s_ktok, 1)
                    for g in range(4):
                        wait(pool, bank_free[a_jobs.banks[A_QT + g]], a_jobs.before(A_QT + g, t) + 1)
                    pool.dma_start(q_d[:, :, bass.ds(t * P, P)].rearrange("h d n -> d h n"), q_feat[:, :, :]).then_inc(s_qst, 16)
                    for g in range(4):
                        wait(pool, bank_free[a_jobs.banks[A_KT + g]], a_jobs.before(A_KT + g, t) + 1)
                    pool.dma_start(k_d[:, :, bass.ds(t * P, P)].rearrange("h d n -> d h n"), k_feat[:, :, :]).then_inc(s_kst, 16)
                if new:
                    t, m, p = new
                    for g in range(2):
                        wait(pool, bank_free[a_jobs.banks[A_U + 2 + g]], a_jobs.before(A_U + 2 + g, t) + 1)
                    pool.dma_start(sz_d[bass.ds(t * P, P), :], sz_out[p][:, :]).then_inc(s_szst[p], 16)
            two_stage(pool, step)

        s_krc = sem("k_rope_copied")

        o = base0 + 32 * KB
        w_o = sb("w_o", [P, KD, D], o); o += 32 * KB
        w_g = sb("w_g", [P, KD, D], o); o += 32 * KB
        w_p = sb("w_p", [P, 2, D], o); o += 8 * KB
        q_s = [sb(f"q_s{p}", [QK, S], o + 4 * KB * p) for p in range(2)]; o += 8 * KB
        k_s = [sb(f"k_s{p}", [QK, S], o + 4 * KB * p) for p in range(2)]; o += 8 * KB
        prob = [sb(f"prob{p}", [P, S], o + 4 * KB * p) for p in range(2)]; o += 8 * KB
        prob_t = [sb(f"prob_t{p}", [P, T, P], o + 4 * KB * p) for p in range(2)]; o += 8 * KB
        o_all = sb("o_all", [P, T, HEADS * VD], o); o += 32 * KB
        assert base_off + o <= 229344, o
        s_jobs = Jobs(base, [0, 2] * 4, HEADS)
        PT = [[4], [5], [4], [5], [4, 5], [4, 5], [4, 5], [4, 5]]
        pt_jobs = Jobs(base, [b for x in PT for b in x], HEADS)
        PT_AT = [sum(len(x) for x in PT[:i]) for i in range(T)]
        o_jobs = Jobs(base, [6, 7] * 4, HEADS)
        s_qin = [sem(f"q_head_in{p}") for p in range(2)]
        s_kin = [sem(f"k_head_in{p}") for p in range(2)]
        s_max = sem("row_max")
        s_exp = sem("row_exp")
        s_rcp = sem("row_sum_inverse")
        s_wo = sem("w_o_in"); s_wg = sem("w_g_in"); s_wp = sem("w_p_in")
        nmax = [stats[:, 20 + p:21 + p] for p in range(2)]
        rsum = [stats[:, 22 + p:23 + p] for p in range(4)]
        rinv = [stats[:, 26 + p:27 + p] for p in range(4)]

        def heads(eng, head, tail):
            head(0, 0, 0, False)
            with eng.Fori(0, (HEADS - 2) // 2) as i:
                head(2 * i + 1, i, 1, True)
                head(2 * i + 2, i + 1, 0, True)
            head(HEADS - 1, HEADS // 2 - 1, 1, True)
            tail()

        def att_sp(sp):
            wait(sp, s_qst, 16 * T)
            wait(sp, s_kst, 16 * T)
            wait(sp, s_phase, PH_A)

            def head(h, m, p, prev):
                if not isinstance(h, int) or h >= 2:
                    wait(sp, bank_full[2], s_jobs.base[2] + 4 * (h - 1))
                sp.dma_start(q_s[p][:, :], q_d[bass.ds(h, 1), :, :].rearrange("h d n -> (h d) n")).then_inc(s_qin[p], 16)
                sp.dma_start(k_s[p][:, :], k_d[bass.ds(h, 1), :, :].rearrange("h d n -> (h d) n")).then_inc(s_kin[p], 16)
                if isinstance(h, int) and h == 0:
                    sp.dma_start(w_o[:, :, :], A["mla_w_out"][0].rearrange("(k p) n -> p k n", p=P)).then_inc(s_wo, 16)
                    sp.dma_start(w_g[:, :, :], A["ple_gate"][0].rearrange("(k p) n -> p k n", p=P)).then_inc(s_wg, 16)
                    sp.dma_start(w_p[:, :, :], A["ple_proj"][0].rearrange("(k p) n -> p k n", p=P)).then_inc(s_wp, 16)
            heads(sp, head, lambda: None)

        def att_pe(pe):
            def scores(h, m, p, i):
                b = s_jobs.banks[i]
                wait(pe, bank_free[b], s_jobs.before(i, h))
                n = (i + 1) * P
                for c in range(0, n, BANK):
                    cn = min(BANK, n - c)
                    mm = pe.matmul(ps[:, b + c // BANK, 0:cn], q_s[p][:, i * P:(i + 1) * P], k_s[p][:, c:c + cn], start=True, stop=True)
                job_end(mm, s_jobs, i)

            def turn(h, i):
                pe.wait_ge(s_exp, 8 * h + i + 1)
                for g in range(len(PT[i])):
                    j = PT_AT[i] + g
                    b = job_start(pe, pt_jobs, j, h)
                    for k in range(4 * g, min(4 * g + 4, i + 1)):
                        mm = pe.transpose(b[:, (k - 4 * g) * P:(k - 4 * g + 1) * P], prob[i % 2][:, k * P:(k + 1) * P], ident)
                    job_end(mm, pt_jobs, j)

            def values(h, i):
                b = job_start(pe, o_jobs, i, h)
                for g in range(len(PT[i])):
                    job_copied(pe, pt_jobs, PT_AT[i] + g, h)
                for k in range(i + 1):
                    mm = pe.matmul(b[:, 0:VD], prob_t[i % 2][:, k, :], v_all[:, k, bass.ds(h * VD, VD)], start=(k == 0), stop=(k == i))
                job_end(mm, o_jobs, i)

            def head(h, m, p, prev):
                pe.wait_ge(s_qin[p], 16 * m + 16)
                pe.wait_ge(s_kin[p], 16 * m + 16)
                for i in range(T):
                    scores(h, m, p, i)
                    if i >= 1:
                        turn(h, i - 1)
                    elif prev:
                        turn(h - 1, T - 1)
                    if i >= 2:
                        values(h, i - 2)
                    elif prev:
                        values(h - 1, T - 2 + i)

            def tail():
                turn(HEADS - 1, T - 1)
                values(HEADS - 1, T - 2)
                values(HEADS - 1, T - 1)
            heads(pe, head, tail)

        def att_dve(v):
            def maxima(h, i):
                b = s_jobs.banks[i]
                v.wait_ge(bank_full[b], s_jobs.before(i, h) + 1)
                n = (i + 1) * P
                flat = ps[:, b:b + 2, :].rearrange("p a n -> p (a n)")
                v.memset(flat[0:64, n - 64:n], -3.0e38).then_inc(s_max, 1)
                v.wait_ge(s_max, 2 * (8 * h + i) + 1)
                v.tensor_reduce(nmax[i % 2], flat[:, 0:n], AX.X, ALU.max, negate=True).then_inc(s_max, 1)

            def copies(h, i):
                b = PT[i][0]
                if b != 4:
                    return
                j = PT_AT[i]
                job_read(v, pt_jobs, j, h)
                wait(v, bank_full[o_jobs.banks[i]], o_jobs.before(i, h))
                n = min(4, i + 1)
                ins = v.tensor_copy(prob_t[i % 2][:, 0:n, :].rearrange("p k n -> p (k n)"), ps[:, 4, 0:n * P])
                job_done(ins, pt_jobs, j)

            def outputs(h, i):
                v.wait_ge(s_exp, 8 * h + i + 1)
                v.reciprocal(rinv[i % 4], rsum[i % 4]).then_inc(s_rcp, 1)
                v.wait_ge(s_rcp, 8 * h + i + 1)
                b = job_read(v, o_jobs, i, h)
                ins = v.tensor_scalar(o_all[:, i, bass.ds(h * VD, VD)], b[:, 0:VD], rinv[i % 4], None, ALU.mult)
                job_done(ins, o_jobs, i)

            def head(h, m, p, prev):
                for i in range(T):
                    maxima(h, i)
                    if i >= 1:
                        copies(h, i - 1)
                    elif prev:
                        copies(h - 1, T - 1)
                    if i >= 2:
                        outputs(h, i - 2)
                    elif prev:
                        outputs(h - 1, T - 2 + i)

            def tail():
                copies(HEADS - 1, T - 1)
                outputs(HEADS - 1, T - 2)
                outputs(HEADS - 1, T - 1)
            v.wait_ge(s_phase, PH_A)
            heads(v, head, tail)

        def att_act(act):
            def exps(h, i):
                b = s_jobs.banks[i]
                act.wait_ge(s_max, 2 * (8 * h + i) + 2)
                n = (i + 1) * P
                flat = ps[:, b:b + 2, :].rearrange("p a n -> p (a n)")
                act.activation(prob[i % 2][:, 0:n], flat[:, 0:n], ACT.Exp, bias=nmax[i % 2], accum_out=rsum[i % 4]).then_inc(s_exp, 1)
                act.wait_ge(s_exp, 8 * h + i + 1)
                act.sem_inc(bank_free[b], 1)

            def copies(h, i):
                b = PT[i][-1]
                if b != 5:
                    return
                j = PT_AT[i] + len(PT[i]) - 1
                job_read(act, pt_jobs, j, h)
                wait(act, bank_full[o_jobs.banks[i]], o_jobs.before(i, h))
                k0 = 4 * (len(PT[i]) - 1)
                n = i + 1 - k0
                ins = act.activation(prob_t[i % 2][:, k0:k0 + n, :].rearrange("p k n -> p (k n)"), ps[:, 5, 0:n * P], ACT.Copy)
                job_done(ins, pt_jobs, j)

            def head(h, m, p, prev):
                for i in range(T):
                    exps(h, i)
                    if i >= 1:
                        copies(h, i - 1)
                    elif prev:
                        copies(h - 1, T - 1)
            act.wait_ge(s_phase, PH_A)
            heads(act, head, lambda: copies(HEADS - 1, T - 1))

        def phase_a_end(pool):
            for b, n in a_ends.items():
                wait(pool, bank_free[b], n)
            wait(pool, s_qst, 16 * T)
            wait(pool, s_kst, 16 * T)
            for p in range(2):
                wait(pool, s_szst[p], 16 * T // 2)
            pool.sem_inc(s_phase, 1)

        a_ends = {b: a_jobs.base[b] + a_jobs.banks.count(b) * T for b in set(a_jobs.banks)}

        h_t = sb("h_t", [P, KD, S], base0)
        o = base0 + 104 * KB
        o_s = [sb(f"o_s{p}", [P, D], o + 4 * KB * p) for p in range(2)]; o += 8 * KB
        sz_in = [sb(f"sz_in{p}", [P, D], o + 4 * KB * p) for p in range(2)]; o += 8 * KB
        res = [sb(f"res{p}", [P, D], o + 4 * KB * p) for p in range(2)]; o += 8 * KB
        o_t = sb("o_t", [P, KD, P], o); o += 4 * KB
        res_t = sb("res_t", [P, KD, P], o); o += 4 * KB
        assert o == base0 + 136 * KB
        o = base0 + 168 * KB
        gate = sb("gate", [P, D], o); o += 4 * KB
        h_tok = [sb(f"h_tok{p}", [P, D], o + 4 * KB * p) for p in range(2)]; o += 8 * KB
        fn_row = sb("fn_row", [P, D], o); o += 4 * KB
        junk_b = sb("junk_b", [P, D], o); o += 4 * KB
        ple_in = [sb(f"ple_in{p}", [P, PLE], o + KB * p) for p in range(2)]; o += 2 * KB
        ple_t = sb("ple_t", [P, 2, P], o); o += KB
        assert base_off + o <= 229344, o
        x1_d = dram("x1_d", (S, D))
        f_jobs = Jobs(base, [0, 1, 5, 0], T)
        g_jobs = Jobs(base, [2, 3, 4, 2, 3, 4, 2], T)
        h_jobs = Jobs(base, [6, 7], T)
        s_szin = [sem(f"sz_in_in{p}") for p in range(2)]
        s_res = [sem(f"res_in{p}") for p in range(2)]
        s_ple = [sem(f"ple_in_in{p}") for p in range(2)]
        s_fn = sem("final_norm_in")
        s_os = sem("o_gated")
        s_x2 = sem("x2_ready")
        s_sq2 = sem("x2_squared")
        s_rs2 = sem("x2_rstd")
        s_x3 = sem("x3_ready")
        s_sq3 = sem("x3_squared"); s_rs3 = sem("x3_rstd")
        s_x1 = sem("x1_ready"); s_sq4 = sem("x1_squared"); s_rs4 = sem("x1_rstd")
        s_h = sem("h_ready")
        s_x1st = [sem(f"x1_stored{p}") for p in range(2)]
        ss2 = stats[:, 30:31]; ms2 = stats[:, 31:32]; rs2 = [stats[:, 32 + p:33 + p] for p in range(2)]
        ss3 = stats[:, 34:35]; ms3 = stats[:, 35:36]; rs3 = stats[:, 36:37]
        ss4 = stats[:, 37:38]; ms4 = stats[:, 38:39]; rs4 = stats[:, 39:40]
        att_last = o_jobs.base[7] + 4 * HEADS

        def b_sp(sp):
            wait(sp, bank_free[7], att_last)
            sp.dma_start(fn_row[:, :], A["final_norm"].partition_broadcast(P)).then_inc(s_fn, 16)

            def step(new, mid, old):
                if new:
                    t, m, p = new
                    later = not isinstance(t, int) or t >= 2
                    if later:
                        wait(sp, s_os, t - 1)
                    sp.dma_start(sz_in[p][:, :], sz_d[bass.ds(t * P, P), :]).then_inc(s_szin[p], 16)
                    if later:
                        wait(sp, bank_full[4], g_jobs.before(2, t) - 3)
                    sp.dma_start(ple_in[p][:, :], A["p"][0, 0, bass.ds(t * P, P), :]).then_inc(s_ple[p], 16)
                    if later:
                        wait(sp, s_x1st[p], 16 * m)
                        wait(sp, s_h, t - 1)
                    sp.dma_start(res[p][:, :], A["x"][0, bass.ds(t * P, P), :]).then_inc(s_res[p], 16)
            three_stage(sp, step)

        def b_pe(pe):
            def step(new, mid, old):
                if new:
                    t, m, p = new
                    pe.wait_ge(s_os, t + 1)
                    for j in range(2):
                        b = job_start(pe, f_jobs, j, t)
                        for k in range(4):
                            mm = pe.transpose(b[:, k * P:(k + 1) * P], o_s[p][:, (4 * j + k) * P:(4 * j + k + 1) * P], ident)
                        job_end(mm, f_jobs, j)
                if mid:
                    t, m, p = mid
                    pe.wait_ge(s_x2, 2 * t + 2)
                    for j in range(2):
                        b = job_start(pe, g_jobs, j, t)
                        for k in range(4):
                            mm = pe.transpose(b[:, k * P:(k + 1) * P], res[p][:, (4 * j + k) * P:(4 * j + k + 1) * P], ident)
                        job_end(mm, g_jobs, j)
                    pe.wait_ge(s_ple[p], 16 * m + 16)
                    b = job_start(pe, g_jobs, 2, t)
                    for k in range(2):
                        mm = pe.transpose(b[:, k * P:(k + 1) * P], ple_in[p][:, k * P:(k + 1) * P], ident)
                    job_end(mm, g_jobs, 2)
                if new:
                    t, m, p = new
                    if isinstance(t, int) and t == 0:
                        pe.wait_ge(s_wo, 16)
                        pe.wait_ge(s_wg, 16)
                        pe.wait_ge(s_wp, 16)
                    for j in range(2):
                        job_copied(pe, f_jobs, j, t)
                    for j in range(2):
                        b = job_start(pe, f_jobs, 2 + j, t)
                        for k in range(KD):
                            mm = pe.matmul(b, o_t[:, k, :], w_o[:, k, j * BANK:(j + 1) * BANK], start=(k == 0), stop=(k == KD - 1))
                        job_end(mm, f_jobs, 2 + j)
                if mid:
                    t, m, p = mid
                    for j in range(3):
                        job_copied(pe, g_jobs, j, t)
                    for j in range(2):
                        b = job_start(pe, g_jobs, 3 + j, t)
                        for k in range(KD):
                            mm = pe.matmul(b, res_t[:, k, :], w_g[:, k, j * BANK:(j + 1) * BANK], start=(k == 0), stop=(k == KD - 1))
                        job_end(mm, g_jobs, 3 + j)
                    for j in range(2):
                        b = job_start(pe, g_jobs, 5 + j, t)
                        for k in range(2):
                            mm = pe.matmul(b, ple_t[:, k, :], w_p[:, k, j * BANK:(j + 1) * BANK], start=(k == 0), stop=(k == 1))
                        job_end(mm, g_jobs, 5 + j)
                if old:
                    t, m, p = old
                    pe.wait_ge(s_h, t + 1)
                    for j in range(2):
                        b = job_start(pe, h_jobs, j, t)
                        for k in range(4):
                            mm = pe.transpose(b[:, k * P:(k + 1) * P], h_tok[p][:, (4 * j + k) * P:(4 * j + k + 1) * P], ident)
                        job_end(mm, h_jobs, j)
            three_stage(pe, step)

        def b_act(act):
            def step(new, mid, old):
                if new:
                    t, m, p = new
                    b = job_read(act, f_jobs, 0, t)
                    job_done(act.activation(o_t[:, 0:4, :].rearrange("p k n -> p (k n)"), b, ACT.Copy), f_jobs, 0)
                if mid:
                    t, m, p = mid
                    b = job_read(act, g_jobs, 0, t)
                    job_done(act.activation(res_t[:, 0:4, :].rearrange("p k n -> p (k n)"), b, ACT.Copy), g_jobs, 0)
                    b = job_read(act, g_jobs, 2, t)
                    job_done(act.activation(ple_t[:, :, :].rearrange("p k n -> p (k n)"), b[:, 0:2 * P], ACT.Copy), g_jobs, 2)
                if old:
                    t, m, p = old
                    act.wait_ge(s_x3, 4 * t + 4)
                    act.activation(junk_b[:, :], res[p][:, :], ACT.Square, accum_out=ss3).then_inc(s_sq3, 1)
                    act.wait_ge(s_x1, t + 1)
                    act.activation(junk_b[:, :], res[p][:, :], ACT.Square, accum_out=ss4).then_inc(s_sq4, 1)
                    act.wait_ge(s_rs4, 2 * t + 2)
                    act.activation(h_tok[p][:, :], res[p][:, :], ACT.Copy, scale=rs4).then_inc(s_h, 1)
                if new:
                    t, m, p = new
                    act.wait_ge(s_x2, 2 * t + 2)
                    act.activation(junk_b[:, :], res[p][:, :], ACT.Square, accum_out=ss2).then_inc(s_sq2, 1)
                if mid:
                    t, m, p = mid
                    act.wait_ge(s_rs2, 2 * t + 2)
                    for j in range(2):
                        b = job_read(act, g_jobs, 3 + j, t)
                        job_done(act.activation(gate[:, j * BANK:(j + 1) * BANK], b, ACT.Sigmoid, scale=rs2[p]), g_jobs, 3 + j)
            three_stage(act, step)

        def b_dve(v):
            def step(new, mid, old):
                if new:
                    t, m, p = new
                    b = job_read(v, f_jobs, 1, t)
                    job_done(v.tensor_copy(o_t[:, 4:8, :].rearrange("p k n -> p (k n)"), b), f_jobs, 1)
                if mid:
                    t, m, p = mid
                    b = job_read(v, g_jobs, 1, t)
                    job_done(v.tensor_copy(res_t[:, 4:8, :].rearrange("p k n -> p (k n)"), b), g_jobs, 1)
                if old:
                    t, m, p = old
                    if isinstance(t, int) and t == 0:
                        v.wait_ge(s_fn, 16)
                    v.wait_ge(s_rs3, 2 * t + 2)
                    v.scalar_tensor_tensor(res[p][:, :], res[p][:, :], rs3, fn_row[:, :], ALU.mult, ALU.mult).then_inc(s_x1, 1)
                if new:
                    t, m, p = new
                    v.wait_ge(s_res[p], 16 * m + 16)
                    for j in range(2):
                        b = job_read(v, f_jobs, 2 + j, t)
                        half = res[p][:, j * BANK:(j + 1) * BANK]
                        v.tensor_tensor(half, b, half, ALU.add).then_inc(s_x2, 1)
                        v.wait_ge(s_x2, 2 * t + j + 1)
                        v.sem_inc(bank_free[f_jobs.banks[2 + j]], 1)
                if mid:
                    t, m, p = mid
                    for j in range(2):
                        v.wait_ge(bank_free[g_jobs.banks[3 + j]], g_jobs.before(3 + j, t) + 1)
                        b = job_read(v, g_jobs, 5 + j, t)
                        half = gate[:, j * BANK:(j + 1) * BANK]
                        v.tensor_tensor(half, b, half, ALU.mult).then_inc(s_x3, 1)
                        v.wait_ge(s_x3, 4 * t + 2 * j + 1)
                        v.sem_inc(bank_free[g_jobs.banks[5 + j]], 1)
                        r = res[p][:, j * BANK:(j + 1) * BANK]
                        v.tensor_tensor(r, r, half, ALU.add).then_inc(s_x3, 1)
                if old:
                    t, m, p = old
                    for j in range(2):
                        b = job_read(v, h_jobs, j, t)
                        ins = v.tensor_tensor(h_t[:, 4 * j:4 * j + 4, bass.ds(t * P, P)], b.rearrange("p (k n) -> p k n", k=4),
                                              bc(gain("attn_norm")[:, 4 * j:4 * j + 4], P), ALU.mult)
                        job_done(ins, h_jobs, j)
            three_stage(v, step)

        def b_pool(pool):
            wait(pool, bank_free[6], o_jobs.base[6] + 4 * HEADS)
            wait(pool, bank_free[7], att_last)

            def step(new, mid, old):
                if new:
                    t, m, p = new
                    wait(pool, s_szin[p], 16 * m + 16)
                    if not isinstance(t, int) or t >= 2:
                        wait(pool, bank_full[1], f_jobs.before(1, t) - 1)
                    pool.tensor_tensor(o_s[p][:, :], o_all[:, bass.ds(t, 1), :].rearrange("p a n -> p (a n)"), sz_in[p][:, :],
                                       ALU.mult).then_inc(s_os, 1)
                if old:
                    t, m, p = old
                    wait(pool, s_sq3, t + 1)
                    rstd(pool, rs3, ms3, ss3, 1, s_rs3, 2 * t, 1.0 / D)
                    wait(pool, s_x1, t + 1)
                    pool.dma_start(x1_d[bass.ds(t * P, P), :], res[p][:, :]).then_inc(s_x1st[p], 16)
                    wait(pool, s_sq4, t + 1)
                    rstd(pool, rs4, ms4, ss4, 1, s_rs4, 2 * t, 1.0 / D)
                if new:
                    t, m, p = new
                    wait(pool, s_sq2, t + 1)
                    rstd(pool, rs2[p], ms2, ss2, 1, s_rs2, 2 * t, 1.0 / D)
            three_stage(pool, step)

        o = base0 + 32 * KB
        w_ch = [sb(f"w_ch{p}", [P, KD, P], o + 4 * KB * p) for p in range(2)]; o += 8 * KB
        w_tk = [sb(f"w_tk{p}", [P, KD, BANK], o + 16 * KB * p) for p in range(2)]; o += 32 * KB
        w_ba = sb("w_ba", [P, KD, 2 * AH], o); ba_lo = sb("ba_lo", [P, KD, 2 * AH], o, F32R); o += 256
        ba_hi = sb("ba_hi", [P, KD, 2 * AH], o, F32R); o += 256
        h_lo = sb("h_lo", [P, KD, S], base0, F32R)
        ch_lo = [sb(f"ch_lo{p}", [P, KD, P], base0 + 32 * KB + 4 * KB * p, F32R) for p in range(2)]
        tk_lo = [sb(f"tk_lo{p}", [P, KD, BANK], base0 + 40 * KB + 16 * KB * p, F32R) for p in range(2)]
        h_hi = sb("h_hi", [P, KD, S], o, F32R); o += 32 * KB
        ch_hi = [sb(f"ch_hi{p}", [P, KD, P], o + 4 * KB * p, F32R) for p in range(2)]; o += 8 * KB
        tk_hi = [sb(f"tk_hi{p}", [P, KD, BANK], o + 16 * KB * p, F32R) for p in range(2)]; o += 32 * KB
        conv_y = [sb(f"conv_y{p}", [P, S], o + 4 * KB * p) for p in range(2)]; o += 8 * KB
        conv_s = [sb(f"conv_s{p}", [P, S], o + 4 * KB * p) for p in range(2)]; o += 8 * KB
        conv_o = [sb(f"conv_o{p}", [P, T, P], o + 4 * KB * p) for p in range(2)]; o += 8 * KB
        tok_o = [sb(f"tok_o{q}", [P, BANK], o + 2 * KB * q) for q in range(4)]; o += 8 * KB
        assert base_off + o <= 229344, o
        C_GATE_A, C_B = CONV_CH, CONV_CH + BANK
        proj_d = dram("proj_d", (S, CONV_CH + 5 * BANK))
        W2_GA = CONV_CH
        W2_BA = W2_GA + AH * HD
        W2_B = W2_BA + 2 * AH
        c_jobs = Jobs(base, [0, 2], CONV_CH // P // 2)
        ct_jobs = Jobs(base, [4, 5, 6, 7], CONV_CH // P // 2)
        NCH = CONV_CH // P
        tk_jobs = Jobs(base, [0, 1, 2, 3, 4, 5, 6, 7], 5)
        ba_jobs = Jobs(base, [0], 1)
        s_wch = [sem(f"w_ch_in{p}") for p in range(2)]
        s_wtk = [sem(f"w_tk_in{p}") for p in range(2)]
        s_wba = sem("w_ba_in")
        s_high = sem("high_parts"); s_low = sem("low_parts")
        CONV_0, H_0, CONV, TOK_0, BA, TOK = 1, 2, KD + 1, KD + NCH + 1, KD + NCH + 2, KD + NCH + 2
        s_cy = sem("conv_taps")
        s_cs = sem("conv_silu")
        s_cst = [sem(f"conv_stored{p}") for p in range(2)]
        s_tst = [sem(f"tok_stored{q}") for q in range(4)]
        w2v = A["w_in_2"][0].rearrange("(k p) n -> p k n", p=P)

        def chunks(eng, chunk):
            with eng.Fori(0, 2) as i:
                chunk(2 * i, i, 0, i * (4 * BANK + 2 * AH), i * (4 * BANK), True)
                chunk(2 * i + 1, i, 1, (BANK + 2 * AH) + i * (2 * BANK), BANK + i * (2 * BANK), False)
            chunk(4, 2, 0, 2 * BANK + 2 * AH, 2 * BANK, False)

        def b_end(pool):
            for b in (6, 7):
                wait(pool, bank_free[b], h_jobs.base[b] + T)
            for p in range(2):
                wait(pool, s_x1st[p], 16 * T // 2)
            pool.sem_inc(s_phase, 1)

        flat = lambda ap: ap.rearrange("p k n -> p (k n)")

        def high(eng, hi, x):
            return eng.activation(hi, x, ACT.Copy)

        def low(v, lo, x, hi):
            return v.tensor_tensor(lo, x, hi.bitcast(F32), ALU.subtract)

        def split_products(pe, out_, pairs, each=None):
            n = 0
            for i, (ah, al, bh, bl) in enumerate(pairs):
                if each:
                    pe.wait_ge(each[0], each[1] + i)
                for a, b_ in ((ah, bl), (al, bh), (ah, bh)):
                    mm = pe.matmul(out_, a, b_, start=(n == 0), stop=(n == 3 * len(pairs) - 1))
                    n += 1
            return mm

        def next_use(m, p):
            return (m, 1) if p == 0 else (m + 1, 0)

        def split_conv(eng, c, m, q):
            if eng.engine == mybir.EngineType.Activation:
                wait(eng, s_wch[q], 16 * m + 16)
                high(eng, flat(ch_hi[q][:, :, :]), flat(w_ch[q][:, :, :])).then_inc(s_high, 1)
            else:
                wait(eng, s_high, CONV_0 if isinstance(c, int) and c == 0 else CONV + c)
                low(eng, ch_lo[q][:, :, :], w_ch[q][:, :, :], ch_hi[q][:, :, :]).then_inc(s_low, 1)

        def split_tok(eng, n, m, q):
            if eng.engine == mybir.EngineType.Activation:
                wait(eng, s_wtk[q], 16 * m + 16)
                high(eng, flat(tk_hi[q][:, :, :]), flat(w_tk[q][:, :, :])).then_inc(s_high, 1)
            else:
                wait(eng, s_high, TOK_0 if isinstance(n, int) and n == 0 else TOK + n)
                low(eng, tk_lo[q][:, :, :], w_tk[q][:, :, :], tk_hi[q][:, :, :]).then_inc(s_low, 1)

        def c_sp(sp):
            wait(sp, s_phase, PH_B)
            sp.dma_start(w_ba[:, :, :], w2v[:, :, W2_BA:W2_B], allow_slow_non_contiguous=True).then_inc(s_wba, 16)

            def step(new, old):
                if new:
                    c, m, p = new
                    if not isinstance(c, int) or c >= 2:
                        wait(sp, bank_full[c_jobs.banks[p]], c_jobs.before(p, m))
                    sp.dma_start(w_ch[p][:, :, :], w2v[:, :, bass.ds(c * P, P)]).then_inc(s_wch[p], 16)
            two_stage(sp, step, NCH)

            def chunk(n, m, p, col, dst, silu):
                if p == 0:
                    wait(sp, bank_full[7], tk_jobs.base[7] + n - 1)
                else:
                    wait(sp, bank_full[7], tk_jobs.base[7] + n - 1)
                src = A["w_in_2"][0].rearrange("(k p) n -> p k n", p=P)
                sp.dma_start(w_tk[p][:, :, :], src[:, :, bass.ds(W2_GA + col, BANK)]).then_inc(s_wtk[p], 16)
            chunks(sp, chunk)

        def c_pe(pe):
            def step(new, old):
                if new:
                    c, m, p = new
                    first = isinstance(c, int) and c == 0
                    wait(pe, s_low, CONV_0 if first else CONV + c)
                    b = c_jobs.banks[p]
                    wait(pe, bank_free[b], c_jobs.before(p, m))
                    for half in range(2):
                        cols = slice(half * BANK, (half + 1) * BANK)
                        mm = split_products(pe, ps[:, b + half, :], each=(s_low, H_0) if first else None, pairs=
                                            [(ch_hi[p][:, k, :], ch_lo[p][:, k, :], h_hi[:, k, cols], h_lo[:, k, cols]) for k in range(KD)])
                    mm.then_inc(bank_full[b], 1)
                if old:
                    c, m, p = old
                    pe.wait_ge(s_cs, c + 1)
                    for j in range(2):
                        b = job_start(pe, ct_jobs, 2 * p + j, m)
                        for k in range(4):
                            mm = pe.transpose(b[:, k * P:(k + 1) * P], conv_s[p][:, (4 * j + k) * P:(4 * j + k + 1) * P], ident)
                        job_end(mm, ct_jobs, 2 * p + j)
            for b in (6, 7):
                pe.wait_ge(bank_free[b], h_jobs.base[b] + T)
            two_stage(pe, step, NCH)

            def chunk(n, m, p, col, dst, silu):
                wait(pe, s_low, TOK + n)
                for t in range(T):
                    b = job_start(pe, tk_jobs, t, n)
                    toks = slice(t * P, (t + 1) * P)
                    mm = split_products(pe, b, [(h_hi[:, k, toks], h_lo[:, k, toks], tk_hi[p][:, k, :], tk_lo[p][:, k, :]) for k in range(KD)])
                    job_end(mm, tk_jobs, t)
            pe.wait_ge(bank_free[0], tk_jobs.base[0]); pe.wait_ge(bank_free[2], tk_jobs.base[2])
            chunks(pe, chunk)
            pe.wait_ge(s_low, BA)
            b = job_start(pe, ba_jobs, 0, 0)
            for t in range(T):
                toks = slice(t * P, (t + 1) * P)
                mm = split_products(pe, b[:, t * 2 * AH:(t + 1) * 2 * AH],
                                    [(h_hi[:, k, toks], h_lo[:, k, toks], ba_hi[:, k, :], ba_lo[:, k, :]) for k in range(KD)])
            job_end(mm, ba_jobs, 0)

        def c_act(act):
            def step(new, old):
                if new:
                    c, m, p = new
                    if not isinstance(c, int) or c + 1 < NCH:
                        split_conv(act, c + 1, *next_use(m, p))
                    b = c_jobs.banks[p]
                    act.wait_ge(bank_full[b], c_jobs.before(p, m) + 1)
                    pair = ps[:, b:b + 2, :].rearrange("p a n -> p (a n)")
                    act.activation(conv_y[p][:, :], pair, ACT.Copy, scale=gain("conv")[:, bass.ds(3 * NCH + c, 1)]).then_inc(s_cy, 1)
                    act.wait_ge(s_cy, 4 * c + 4)
                    act.activation(conv_s[p][:, :], conv_y[p][:, :], ACT.Silu).then_inc(s_cs, 1)
                if old:
                    c, m, p = old
                    wait(act, s_cst[p], 16 * m)
                    for j in range(2):
                        b = job_read(act, ct_jobs, 2 * p + j, m)
                        job_done(act.activation(conv_o[p][:, 4 * j:4 * j + 4, :].rearrange("p k n -> p (k n)"), b, ACT.Copy),
                                 ct_jobs, 2 * p + j)
            act.wait_ge(s_phase, PH_B)
            split_conv(act, 0, 0, 0)
            for k in range(KD):
                high(act, h_hi[:, k, :], h_t[:, k, :]).then_inc(s_high, 1)
            two_stage(act, step, NCH)
            split_tok(act, 0, 0, 0)
            act.wait_ge(s_wba, 16)
            high(act, flat(ba_hi[:, :, :]), flat(w_ba[:, :, :])).then_inc(s_high, 1)

            def chunk(n, m, p, col, dst, silu):
                for t in range(0, T, 1 if silu else 2):
                    q = t % 4
                    uses = tok_uses(n, m, t, p)
                    wait(act, s_tst[q], 16 * uses)
                    b = job_read(act, tk_jobs, t, n)
                    job_done(act.activation(tok_o[q][:, :], b, ACT.Silu if silu else ACT.Copy), tk_jobs, t)
                    if t in (2, 3) and not (isinstance(n, int) and n == 4) and (silu == (t == 3)):
                        split_tok(act, n + 1, *next_use(m, p))
            chunks(act, chunk)

        def tok_uses(n, m, t, p):
            return 2 * n + t // 4

        def c_dve(v):
            def step(new, old):
                if new:
                    c, m, p = new
                    if not isinstance(c, int) or c + 1 < NCH:
                        split_conv(v, c + 1, *next_use(m, p))
                    b = c_jobs.banks[p]
                    pair = ps[:, b:b + 2, :].rearrange("p a n -> p (a n)")
                    for i in range(1, TAPS):
                        v.wait_ge(s_cy, 4 * c + i)
                        ins = v.scalar_tensor_tensor(conv_y[p][:, i:], pair[:, 0:S - i], gain("conv")[:, bass.ds((3 - i) * NCH + c, 1)],
                                                     conv_y[p][:, i:], ALU.mult, ALU.add)
                        ins.then_inc(s_cy, 1)
                    v.wait_ge(s_cy, 4 * c + 4)
                    v.sem_inc(bank_free[b], 1)
            v.wait_ge(s_phase, PH_B)
            split_conv(v, 0, 0, 0)
            for k in range(KD):
                v.wait_ge(s_high, H_0 + k)
                low(v, h_lo[:, k, :], h_t[:, k, :], h_hi[:, k, :]).then_inc(s_low, 1)
            two_stage(v, step, NCH)
            split_tok(v, 0, 0, 0)
            v.wait_ge(s_high, BA)
            low(v, ba_lo[:, :, :], w_ba[:, :, :], ba_hi[:, :, :]).then_inc(s_low, 1)

            def chunk(n, m, p, col, dst, silu):
                if not (isinstance(n, int) and n == 4):
                    split_tok(v, n + 1, *next_use(m, p))
                if silu:
                    return
                for t in range(1, T, 2):
                    q = t % 4
                    wait(v, s_tst[q], 16 * tok_uses(n, m, t, p))
                    b = job_read(v, tk_jobs, t, n)
                    job_done(v.tensor_copy(tok_o[q][:, :], b), tk_jobs, t)
            chunks(v, chunk)
            b = job_read(v, ba_jobs, 0, 0)
            job_done(v.tensor_copy(ba[:, :, :].rearrange("p t n -> p (t n)"), b[:, 0:T * 2 * AH]), ba_jobs, 0)

        def c_pool(pool):
            def step(new, old):
                if old:
                    c, m, p = old
                    for j in range(2):
                        wait(pool, bank_free[ct_jobs.banks[2 * p + j]], ct_jobs.before(2 * p + j, m) + 1)
                    pool.dma_start(proj_d[:, bass.ds(c * P, P)].rearrange("(t p) n -> p t n", p=P), conv_o[p][:, :, :]).then_inc(s_cst[p], 16)
            two_stage(pool, step, NCH)

            def chunk(n, m, p, col, dst, silu):
                for t in range(T):
                    wait(pool, bank_free[tk_jobs.banks[t]], tk_jobs.before(t, n) + 1)
                    pool.dma_start(proj_d[t * P:(t + 1) * P, bass.ds(C_GATE_A + dst, BANK)], tok_o[t % 4][:, :]).then_inc(s_tst[t % 4], 16)
            chunks(pool, chunk)
            for p in range(2):
                wait(pool, s_cst[p], 16 * NCH // 2)
            for q in range(4):
                wait(pool, s_tst[q], 16 * 10)
            wait(pool, bank_free[0], ba_jobs.base[0] + 1)
            pool.sem_inc(s_phase, 1)


        NA, NB_ = AH * HD, BH * HD
        o = base0
        w_o2 = sb("w_o2", [P, KD, D], o); o += 32 * KB
        w_r = sb("w_r", [P, KD, GROUPS + EXPERTS], o); o += KD * (GROUPS + EXPERTS) * 4
        gates = sb("gates", [P, 16, T * AH], o); o += 2 * KB
        qkv_in = [sb(f"qkv_in{p}", [P, 3 * NA], o + 6 * KB * p) for p in range(2)]; o += 12 * KB
        tk_in = [sb(f"tk_in{p}", [P, 5 * BANK], o + 10 * KB * p) for p in range(2)]; o += 20 * KB
        rot = sb("rot", [P, T, HD], o); o += 4 * KB
        na_row = sb("na_row", [P, HD], o); o += 512
        nb_row = sb("nb_row", [P, NB_], o); o += 2 * KB
        gate_rows = sb("gate_rows", [P, 2, AH], o); o += 32

        def heads4(name, n=1, h=4):
            nonlocal o
            r = [sb(f"{name}{q}", [P, h, HD], o + h * 512 * q) for q in range(n)]
            o += h * 512 * n
            return r if n > 1 else r[0]

        k_t, q_t, u_fin, attn_t, v_b, k_d2 = (heads4(x, 2) for x in ("k_t", "q_t", "u_fin", "attn_t", "v_b", "k_d2"))
        x_lev = heads4("x_lev", 2)
        qk_n = heads4("qk_n", 1, 8)
        qk_sq = heads4("qk_sq", 1, 8)
        qk_r = heads4("qk_r", 2, 8)
        g_n = heads4("g_n", 2, 8)
        o_cat = heads4("o_cat", 1, 8)
        o_sq = heads4("o_sq", 1, 8)
        mixed = heads4("mixed", 2, 8)
        tri_g, diff, d_max, d_min, e_low, e_up, e_b, e_m, a_mat = (heads4(x) for x in
            ("tri_g", "diff", "d_max", "d_min", "e_low", "e_up", "e_b", "e_m", "a_mat"))
        cos_x, sin_x = heads4("cos_x", 1, 8), heads4("sin_x", 1, 8)
        t_w, u_w, y_w, rhs, v_new, s_a, s_ad = (heads4(x) for x in ("t_w", "u_w", "y_w", "rhs", "v_new", "s_a", "s_ad"))
        qb_t, kb_t, p_t, k_dk, s_b, s_bd = (heads4(x) for x in ("qb_t", "kb_t", "p_t", "k_dk", "s_b", "s_bd"))
        assert base_off + o <= 229344, (o, base_off + o - 229344)
        mixed_d = dram("mixed_d", (S, D))

        def col(n):
            return stats[:, n:n + 8]
        ms_o, rs_o, ss_o = (col(40 + 8 * i) for i in range(3))
        ms_qk, rs_qk, ss_qk = ([col(at + 8 * p) for p in range(2)] for at in (64, 98, 114 - 2))

        class Count:

            def __init__(self, name, names, after=None):
                self.sem = after.sem if after else sem(name)
                self.names, self.base = names.split(), after.base + T * len(after.names) if after else 0

            def done(self, ins, name):
                assert name in self.names, name
                ins.then_inc(self.sem, 1)

            def wait(self, eng, name, t):
                wait(eng, self.sem, t * len(self.names) + (self.base + self.names.index(name) + 1))

        (G_BETA, G_EA, G_X, G_NX, G_E, G_SP, G_G, G_GC, G_GL, G_D, G_EGC, G_EKD, G_EGL, G_NBE) = range(14)
        gs = lambda i: gates[:, i, :]
        gt = lambda i, t: gates[:, i, bass.ds(t * AH, AH)]
        s_din = sem("d_tables_in")
        s_gact = sem("gate_act"); s_gdve = sem("gate_dve")
        s_zero = sem("states_zero")
        s_ldA = [sem(f"qkv_in_in{p}") for p in range(2)]
        s_ldB = [sem(f"tk_in_in{p}") for p in range(2)]
        s_mst = [sem(f"mixed_stored{p}") for p in range(2)]
        s_wo2 = sem("w_o2_in"); s_wr = sem("w_r_in")
        gc_jobs = Jobs(base, [0], 1)
        LEV = 7
        N_KQ, N_B, N_KK, N_QK, N_X0, N_LEV = 0, 2, 3, 4, 5, 6
        n_jobs = Jobs(base, [j % 4 for j in range(N_LEV + 3 * (LEV - 1) - 1)], T)
        O_KS, O_QS, O_VN, O_AV, O_ST, O_TQ, O_TK, O_SB, O_IN, O_CR, O_SR = range(11)
        r_jobs = Jobs(base, [4, 5, 6, 7, 4, 5, 6, 7, 4, 5, 6], T)
        pool_n = Count("d_pool_new", "trig vb kd eb em x0 x1 x2 cosx x3 sinx x4 rotlo rot x5 x6 gna gnb")
        dve_n = Count("d_dve_new", "qkn dmax dmin t0")
        act_n = Count("d_act_new", "e_low e_up")
        act_a = Count("d_act_ahead", "sq"); dve_a = Count("d_dve_ahead", "sums"); pool_a = Count("d_pool_ahead", "ms rs rsq")
        pool_o = Count("d_pool_old", "sad kdk sbd ms rs")
        dve_o = Count("d_dve_old", "r1 r o1 o2 ob1 ob sumo on mixed")
        act_o = Count("d_act_old", "osq")

        def d0_sp(sp):
            wait(sp, s_phase, PH_C)
            sp.dma_start(gate_rows[:, 0, :], A["a_log_2"][0].partition_broadcast(P)).then_inc(s_din, 16)
            sp.dma_start(gate_rows[:, 1, :], A["dt_bias_2"][0].partition_broadcast(P)).then_inc(s_din, 16)
            sp.dma_start(rot[:, :, :], A["c_rot"].rearrange("(t p) n -> p t n", p=P)).then_inc(s_din, 16)
            sp.dma_start(na_row[:, :], A["norm_a_2"][0].partition_broadcast(P)).then_inc(s_din, 16)
            sp.dma_start(nb_row[:, :], A["norm_b_2"][0].partition_broadcast(P)).then_inc(s_din, 16)

            def step(new, old):
                if new:
                    t, m, p = new
                    later = not isinstance(t, int) or t >= 2
                    if later:
                        dve_n.wait(sp, "qkn", t - 2)
                        pool_n.wait(sp, "vb", t - 2)
                    sp.dma_start(qkv_in[p][:, :], proj_d[bass.ds(t * P, P), 0:3 * NA]).then_inc(s_ldA[p], 16)
                    if later:
                        pool_n.wait(sp, "gnb", t - 2)
                        wait(sp, bank_full[6], r_jobs.before(O_SR, t - 2) + 1)
                    sp.dma_start(tk_in[p][:, :], proj_d[bass.ds(t * P, P), 3 * NA:]).then_inc(s_ldB[p], 16)
                    if isinstance(t, int) and t == 0:
                        sp.dma_start(w_o2[:, :, :], A["w_out_2"][0].rearrange("(k p) n -> p k n", p=P)).then_inc(s_wo2, 16)
                        sp.dma_start(w_r[:, :, 0:GROUPS], A["w_router_group_2"][0].rearrange("(k p) n -> p k n", p=P)).then_inc(s_wr, 16)
                        sp.dma_start(w_r[:, :, GROUPS:], A["w_router_expert_2"][0].rearrange("(k p) n -> p k n", p=P)).then_inc(s_wr, 16)
            two_stage_from1(sp, step)

        def d0_act(act):
            g3 = lambda i: gs(i).rearrange("p (t h) -> p t h", t=T)
            act.wait_ge(s_phase, PH_C)
            act.activation(g3(G_BETA), ba[:, :, 0:AH], ACT.Sigmoid).then_inc(s_gact, 1)
            act.wait_ge(s_din, 80)
            act.activation(gates[:, G_EA, 0:AH], gate_rows[:, 0, :], ACT.Exp).then_inc(s_gact, 1)
            act.wait_ge(s_gdve, 3)
            act.activation(gs(G_E), gs(G_NX), ACT.Exp, scale=-1.0).then_inc(s_gact, 1)
            act.wait_ge(s_gdve, 4)
            act.activation(gs(G_SP), gs(G_E), ACT.Ln).then_inc(s_gact, 1)
            act.wait_ge(s_gdve, 9)
            act.activation(gs(G_EGC), gs(G_GC), ACT.Exp).then_inc(s_gact, 1)
            act.activation(gs(G_EGL), gs(G_GL), ACT.Exp).then_inc(s_gact, 1)
            act.activation(gs(G_EKD), gs(G_D), ACT.Exp).then_inc(s_gact, 1)

        def d0_dve(v):
            g3 = lambda i: gs(i).rearrange("p (t h) -> p t h", t=T)
            n = 0

            def link(ins):
                nonlocal n
                n += 1
                ins.then_inc(s_gdve, 1)
                v.wait_ge(s_gdve, n)
            v.wait_ge(s_phase, PH_C)
            v.wait_ge(s_din, 80)
            link(v.tensor_tensor(g3(G_X), ba[:, :, AH:], bc1(gate_rows[:, 1, :], T), ALU.add))
            link(v.tensor_scalar(gs(G_NX), gs(G_X), -1.0, None, ALU.mult))
            link(v.tensor_tensor(gs(G_NX), gs(G_NX), gs(G_X), ALU.max))
            v.wait_ge(s_gact, 3)
            link(v.tensor_scalar(gs(G_E), gs(G_E), 1.0, None, ALU.add))
            v.wait_ge(s_gact, 4)
            link(v.scalar_tensor_tensor(gs(G_SP), gs(G_X), 0.0, gs(G_SP), ALU.max, ALU.add))
            link(v.scalar_tensor_tensor(g3(G_G), g3(G_SP), -1.0, bc1(gates[:, G_EA, 0:AH], T), ALU.mult, ALU.mult))
            b = job_read(v, gc_jobs, 0, 0)
            link(v.tensor_copy(gates[:, G_GC:G_GC + 2, :].rearrange("p a n -> p (a n)"), b[:, 0:2 * T * AH]))
            link(v.tensor_tensor(gs(G_D), gs(G_GL), gs(G_GC), ALU.subtract))
            job_done(v.tensor_scalar(gs(G_NX), gs(G_X), 1.0, None, ALU.mult), gc_jobs, 0)
            v.sem_inc(s_gdve, 1); n += 1
            v.wait_ge(s_gact, 7)
            link(v.scalar_tensor_tensor(gs(G_NBE), gs(G_BETA), -1.0, gs(G_EGC), ALU.mult, ALU.mult))

        def d0_pe(pe):
            pe.wait_ge(s_gdve, 6)
            b = job_start(pe, gc_jobs, 0, 0)
            pe.matmul(b[:, 0:T * AH], tri, gs(G_G), start=True, stop=True)
            job_end(pe.matmul(b[:, T * AH:2 * T * AH], ones, gs(G_G), start=True, stop=True), gc_jobs, 0)

        def q4(b):
            return b.rearrange("p (h n) -> p h n", h=4)

        ORDER = ("n_norm o_state_read n_turn n_decay o_new_values n_scores n_first o_values_out n_level1 o_turn "
                 "n_level2 o_scores n_level3 ahead o_mix n_level4 o_square n_level5 o_end n_level6").split()

        def d_steps(eng, pieces):
            def ahead(t, m, p):
                if "ahead" in pieces:
                    pieces["ahead"](t, m, p)

            def step(new, old):
                for name in ORDER:
                    if name == "ahead":
                        if new and (not isinstance(new[0], int) or new[0] + 1 < T):
                            ahead(new[0] + 1, *next_use(new[1], new[2]))
                        continue
                    tile = new if name[0] == "n" else old
                    if tile and name in pieces:
                        pieces[name](*tile)
            ahead(0, 0, 0)
            two_stage(eng, step)

        def lev_job(s, which):
            return N_LEV + 3 * (s - 1) + which

        def d_pe(pe):
            def four(jobs, j, t, lhs, rhs_):
                b = job_start(pe, jobs, j, t)
                for h in range(4):
                    mm = pe.matmul(b[:, h * HD:(h + 1) * HD], lhs[:, h, :], rhs_[:, h, :], start=True, stop=True)
                job_end(mm, jobs, j)

            def turn4(jobs, j, t, src):
                b = job_start(pe, jobs, j, t)
                for h in range(4):
                    mm = pe.transpose(b[:, h * HD:(h + 1) * HD], src[:, h, :], ident)
                job_end(mm, jobs, j)

            def n_turn(t, m, p):
                dve_n.wait(pe, "qkn", t)
                turn4(n_jobs, N_KQ, t, qk_n[:, 0:4, :])
                turn4(n_jobs, N_KQ + 1, t, qk_n[:, 4:8, :])

            def n_decay(t, m, p):
                pool_n.wait(pe, "trig", t)
                b = job_start(pe, n_jobs, N_B, t)
                job_end(pe.matmul(b, ones, tri_g[:, :, :].rearrange("p h n -> p (h n)"), start=True, stop=True), n_jobs, N_B)

            def n_scores(t, m, p):
                job_copied(pe, n_jobs, N_KQ, t)
                job_copied(pe, n_jobs, N_KQ + 1, t)
                four(n_jobs, N_KK, t, k_t[p], k_t[p])
                four(n_jobs, N_QK, t, k_t[p], q_t[p])

            def n_first(t, m, p):
                pool_n.wait(pe, "x0", t)
                turn4(n_jobs, N_X0, t, x_lev[0])

            def level(s):
                def piece(t, m, p):
                    pool_n.wait(pe, f"x{s}", t)
                    if s == 1:
                        job_copied(pe, n_jobs, N_X0, t)
                    else:
                        job_copied(pe, n_jobs, lev_job(s - 1, 1), t)
                    four(n_jobs, lev_job(s, 0), t, x_lev[s % 2], u_w)
                    job_copied(pe, n_jobs, lev_job(s, 0), t)
                    if s == 1:
                        dve_n.wait(pe, "t0", t)
                    else:
                        job_copied(pe, n_jobs, lev_job(s - 1, 2), t)
                    four(n_jobs, lev_job(s, 1), t, t_w, y_w)
                    if s < LEV - 1:
                        four(n_jobs, lev_job(s, 2), t, y_w, t_w)
                return piece

            def o_state_read(t, m, p):
                job_copied(pe, r_jobs, O_ST, t - 1)
                four(r_jobs, O_KS, t, k_t[p], s_a)
                four(r_jobs, O_QS, t, q_t[p], s_a)

            def o_new_values(t, m, p):
                dve_o.wait(pe, "r", t)
                four(r_jobs, O_VN, t, u_fin[p], rhs)

            def o_values_out(t, m, p):
                job_copied(pe, r_jobs, O_VN, t)
                four(r_jobs, O_AV, t, attn_t[p], v_new)
                four(r_jobs, O_ST, t, k_d2[p], v_new)

            def o_turn(t, m, p):
                turn4(r_jobs, O_TQ, t, qk_r[p][:, 0:4, :])
                turn4(r_jobs, O_TK, t, qk_r[p][:, 4:8, :])

            def o_scores(t, m, p):
                job_copied(pe, r_jobs, O_TQ, t)
                job_copied(pe, r_jobs, O_TK, t)
                four(r_jobs, O_SB, t, kb_t, qb_t)

            def o_mix(t, m, p):
                job_copied(pe, r_jobs, O_SB, t)
                vals = tk_in[p][:, 3 * BANK:4 * BANK].rearrange("p (h n) -> p h n", h=4)
                pe.wait_ge(s_ldB[p], 16 * m + 16)
                four(r_jobs, O_IN, t, p_t, vals)
                job_copied(pe, r_jobs, O_SR, t - 1)
                four(r_jobs, O_CR, t, qb_t, s_b)
                pool_o.wait(pe, "kdk", t)
                four(r_jobs, O_SR, t, k_dk, vals)
            pe.wait_ge(s_zero, 2)
            pieces = dict(n_turn=n_turn, n_decay=n_decay, n_scores=n_scores, n_first=n_first, o_state_read=o_state_read,
                          o_new_values=o_new_values, o_values_out=o_values_out, o_turn=o_turn, o_scores=o_scores, o_mix=o_mix)
            for s in range(1, LEV):
                pieces[f"n_level{s}"] = level(s)
            d_steps(pe, pieces)

        def d_act(act):
            def copy(jobs, j, t, dst):
                b = job_read(act, jobs, j, t)
                job_done(act.activation(dst[:, :, :].rearrange("p h n -> p (h n)"), b, ACT.Copy), jobs, j)

            def ahead(t, m, p):
                act.wait_ge(s_ldA[p], 16 * m + 16)
                if not isinstance(t, int) or t > 0:
                    dve_a.wait(act, "sums", t - 1)
                act_a.done(act.activation(qk_sq[:, :, :].rearrange("p h n -> p (h n)"), qkv_in[p][:, 0:2 * NA], ACT.Square), "sq")

            def n_turn(t, m, p):
                copy(n_jobs, N_KQ, t, q_t[p])

            def n_scores(t, m, p):
                dve_n.wait(act, "dmax", t)
                act_n.done(act.activation(e_low[:, :, :], d_max[:, :, :], ACT.Exp, scale=-1.0), "e_low")
                dve_n.wait(act, "dmin", t)
                act_n.done(act.activation(e_up[:, :, :], d_min[:, :, :], ACT.Exp), "e_up")

            def level(s):
                return lambda t, m, p: copy(n_jobs, lev_job(s, 0), t, y_w)

            def o_new_values(t, m, p):
                copy(r_jobs, O_VN, t, v_new)

            def o_turn(t, m, p):
                copy(r_jobs, O_TQ, t, qb_t)

            def o_square(t, m, p):
                dve_o.wait(act, "ob", t)
                act_o.done(act.activation(o_sq[:, :, :], o_cat[:, :, :], ACT.Square), "osq")
            pieces = dict(ahead=ahead, n_turn=n_turn, n_scores=n_scores, o_new_values=o_new_values, o_turn=o_turn, o_square=o_square)
            for s in range(1, LEV):
                pieces[f"n_level{s}"] = level(s)
            d_steps(act, pieces)

        def d_dve(v):
            def ahead(t, m, p):
                act_a.wait(v, "sq", t)
                dve_a.done(v.tensor_reduce(ss_qk[p], qk_sq[:, :, :], AX.X, ALU.add), "sums")

            def n_norm(t, m, p):
                pool_a.wait(v, "rsq", t)
                v.wait_ge(s_ldA[p], 16 * m + 16)
                dve_n.done(v.tensor_tensor(qk_n[:, :, :], qkv_in[p][:, 0:2 * NA].rearrange("p (h n) -> p h n", h=8),
                                           bc(rs_qk[p], HD), ALU.mult), "qkn")

            def n_turn(t, m, p):
                b = job_read(v, n_jobs, N_KQ + 1, t)
                job_done(v.tensor_copy(k_t[p][:, :, :].rearrange("p h n -> p (h n)"), b), n_jobs, N_KQ + 1)

            def n_decay(t, m, p):
                b = job_read(v, n_jobs, N_B, t)
                job_done(v.tensor_tensor(diff[:, :, :], q4(b), bc(gt(G_GC, t), HD), ALU.subtract), n_jobs, N_B)
                v.wait_ge(bank_free[n_jobs.banks[N_B]], n_jobs.before(N_B, t) + 1)
                dve_n.done(v.tensor_scalar(d_max[:, :, :], diff[:, :, :], 0.0, None, ALU.max), "dmax")
                dve_n.done(v.tensor_scalar(d_min[:, :, :], diff[:, :, :], 0.0, None, ALU.min), "dmin")

            def n_scores(t, m, p):
                pool_n.wait(v, "eb", t)
                b = job_read(v, n_jobs, N_KK, t)
                job_done(v.tensor_tensor(a_mat[:, :, :], q4(b), e_b[:, :, :], ALU.mult), n_jobs, N_KK)
                pool_n.wait(v, "em", t)
                b = job_read(v, n_jobs, N_QK, t)
                job_done(v.tensor_tensor(attn_t[p][:, :, :], q4(b), e_m[:, :, :], ALU.mult), n_jobs, N_QK)

            def n_first(t, m, p):
                pool_n.wait(v, "x0", t)
                dve_n.done(v.tensor_tensor(t_w[:, :, :], bc1(ident, 4), x_lev[0][:, :, :], ALU.subtract), "t0")
                b = job_read(v, n_jobs, N_X0, t)
                job_done(v.tensor_tensor(u_w[:, :, :], bc1(ident, 4), q4(b), ALU.subtract), n_jobs, N_X0)

            def level(s):
                def piece(t, m, p):
                    b = job_read(v, n_jobs, lev_job(s, 1), t)
                    if s == 1:
                        job_copied(v, n_jobs, N_X0, t)
                    else:
                        job_copied(v, n_jobs, lev_job(s - 1, 1), t)
                    dst = u_w if s < LEV - 1 else u_fin[p]
                    job_done(v.tensor_tensor(dst[:, :, :], u_w[:, :, :], q4(b), ALU.subtract), n_jobs, lev_job(s, 1))
                    if s < LEV - 1:
                        b = job_read(v, n_jobs, lev_job(s, 2), t)
                        if s == 1:
                            dve_n.wait(v, "t0", t)
                        else:
                            job_copied(v, n_jobs, lev_job(s - 1, 2), t)
                        job_done(v.tensor_tensor(t_w[:, :, :], t_w[:, :, :], q4(b), ALU.subtract), n_jobs, lev_job(s, 2))
                return piece

            def o_state_read(t, m, p):
                b = job_read(v, r_jobs, O_KS, t)
                dve_o.done(v.tensor_tensor(rhs[:, :, :], q4(b), bc(gt(G_NBE, t), HD), ALU.mult), "r1")
                dve_o.wait(v, "r1", t)
                v.sem_inc(bank_free[r_jobs.banks[O_KS]], 1)
                dve_o.done(v.tensor_tensor(rhs[:, :, :], rhs[:, :, :], v_b[p][:, :, :], ALU.add), "r")
                b = job_read(v, r_jobs, O_QS, t)
                dve_o.done(v.tensor_tensor(o_cat[:, 0:4, :], q4(b), bc(gt(G_EGC, t), HD), ALU.mult), "o1")
                dve_o.wait(v, "o1", t)
                v.sem_inc(bank_free[r_jobs.banks[O_QS]], 1)

            def o_values_out(t, m, p):
                b = job_read(v, r_jobs, O_AV, t)
                dve_o.done(v.tensor_tensor(o_cat[:, 0:4, :], o_cat[:, 0:4, :], q4(b), ALU.add), "o2")
                dve_o.wait(v, "o2", t)
                v.sem_inc(bank_free[r_jobs.banks[O_AV]], 1)
                pool_o.wait(v, "sad", t)
                b = job_read(v, r_jobs, O_ST, t)
                job_done(v.tensor_tensor(s_a[:, :, :], s_ad[:, :, :], q4(b), ALU.add), r_jobs, O_ST)

            def o_turn(t, m, p):
                b = job_read(v, r_jobs, O_TK, t)
                job_done(v.tensor_copy(kb_t[:, :, :].rearrange("p h n -> p (h n)"), b), r_jobs, O_TK)

            def o_scores(t, m, p):
                b = job_read(v, r_jobs, O_SB, t)
                job_done(v.tensor_tensor(p_t[:, :, :], q4(b), q4(const("decay")), ALU.mult), r_jobs, O_SB)

            def o_mix(t, m, p):
                b = job_read(v, r_jobs, O_CR, t)
                dve_o.done(v.tensor_tensor(o_cat[:, 4:8, :], q4(b), bc(const("qdec"), HD), ALU.mult), "ob1")
                dve_o.wait(v, "ob1", t)
                v.sem_inc(bank_free[r_jobs.banks[O_CR]], 1)
                b = job_read(v, r_jobs, O_IN, t)
                dve_o.done(v.tensor_tensor(o_cat[:, 4:8, :], o_cat[:, 4:8, :], q4(b), ALU.add), "ob")
                dve_o.wait(v, "ob", t)
                v.sem_inc(bank_free[r_jobs.banks[O_IN]], 1)
                pool_o.wait(v, "sbd", t)
                b = job_read(v, r_jobs, O_SR, t)
                job_done(v.tensor_tensor(s_b[:, :, :], s_bd[:, :, :], q4(b), ALU.add), r_jobs, O_SR)

            def o_end(t, m, p):
                act_o.wait(v, "osq", t)
                dve_o.done(v.tensor_reduce(ss_o, o_sq[:, :, :], AX.X, ALU.add), "sumo")
                pool_o.wait(v, "rs", t)
                dve_o.done(v.tensor_tensor(o_cat[:, :, :], o_cat[:, :, :], bc(rs_o, HD), ALU.mult), "on")
                dve_o.wait(v, "on", t)
                pool_n.wait(v, "gnb", t)
                wait(v, s_mst[p], 16 * m)
                dve_o.done(v.tensor_tensor(mixed[p][:, :, :], o_cat[:, :, :], g_n[p][:, :, :], ALU.mult), "mixed")
            pieces = dict(ahead=ahead, n_norm=n_norm, n_turn=n_turn, n_decay=n_decay, n_scores=n_scores, n_first=n_first,
                          o_state_read=o_state_read, o_values_out=o_values_out, o_turn=o_turn, o_scores=o_scores, o_mix=o_mix, o_end=o_end)
            for s in range(1, LEV):
                pieces[f"n_level{s}"] = level(s)
            d_steps(v, pieces)

        def d_pool(pool):
            tt = pool.tensor_tensor

            def ahead(t, m, p):
                dve_a.wait(pool, "sums", t)
                pool_a.done(pool.tensor_scalar(ms_qk[p], ss_qk[p], EPS, None, ALU.add), "ms")
                pool_a.wait(pool, "ms", t)
                pool_a.done(tt(rs_qk[p], ms_qk[p], neghalf[:, 0:8], ALU.pow), "rs")
                pool_a.wait(pool, "rs", t)
                pool_a.done(pool.tensor_scalar(rs_qk[p][:, 0:AH], rs_qk[p][:, 0:AH], HD ** -0.5, None, ALU.mult), "rsq")

            def n_norm(t, m, p):
                pool_n.done(tt(tri_g[:, :, :], bc1(tri, 4), bc(gt(G_G, t), HD), ALU.mult), "trig")

            def n_turn(t, m, p):
                wait(pool, bank_full[n_jobs.banks[N_KQ + 1]], n_jobs.before(N_KQ + 1, t) + 1)
                vals = qkv_in[p][:, 2 * NA:].rearrange("p (h n) -> p h n", h=4)
                pool_n.done(tt(v_b[p][:, :, :], vals, bc(gt(G_BETA, t), HD), ALU.mult), "vb")
                dve_n.wait(pool, "qkn", t)
                pool_n.done(tt(k_d2[p][:, :, :], qk_n[:, 4:8, :], bc(gt(G_EKD, t), HD), ALU.mult), "kd")

            half = HD // 2

            def by_table(t, p, dst, c0, name):
                x = tk_in[p][:, BANK:3 * BANK].rearrange("p (h n) -> p h n", n=half)
                pool_n.done(tt(dst[:, :, :].rearrange("p h (a n) -> p (h a) n", a=2), x,
                               rot[:, bass.ds(t, 1), c0:c0 + half].to_broadcast([P, 16, half]), ALU.mult), name)

            def n_rotate(s, t, m, p):
                if s == 1:
                    wait(pool, s_ldB[p], 16 * m + 16)
                    by_table(t, p, cos_x, 0, "cosx")
                if s == 2:
                    by_table(t, p, sin_x, half, "sinx")
                if s == 3:
                    pool_n.wait(pool, "sinx", t)
                    pool_n.done(tt(qk_r[p][:, :, 0:half], cos_x[:, :, 0:half], sin_x[:, :, half:], ALU.subtract), "rotlo")
                    pool_n.done(tt(qk_r[p][:, :, half:], sin_x[:, :, 0:half], cos_x[:, :, half:], ALU.add), "rot")

            def n_scores(t, m, p):
                act_n.wait(pool, "e_low", t)
                pool_n.done(tt(e_b[:, :, :], e_low[:, :, :], bc(gt(G_BETA, t), HD), ALU.mult), "eb")
                act_n.wait(pool, "e_up", t)
                pool_n.done(tt(e_m[:, :, :], e_up[:, :, :], bc1(tri, 4), ALU.mult), "em")

            def x_level(s, t):
                mask = const("levels")[:, s * P:(s + 1) * P]
                pool_n.done(tt(x_lev[s % 2][:, :, :], a_mat[:, :, :], bc1(mask, 4), ALU.mult), f"x{s}")

            def n_first(t, m, p):
                job_copied(pool, n_jobs, N_KK, t)
                x_level(0, t)
                x_level(1, t)

            def level(s):
                def piece(t, m, p):
                    if s == 1:
                        job_copied(pool, n_jobs, N_X0, t)
                    else:
                        wait(pool, bank_full[n_jobs.banks[lev_job(s - 1, 0)]], n_jobs.before(lev_job(s - 1, 0), t) + 1)
                    x_level(s + 1, t)
                    n_rotate(s, t, m, p)
                return piece

            def n_gates(t, m, p):
                ga = tk_in[p][:, 0:BANK].rearrange("p (h n) -> p h n", h=4)
                pool_n.done(tt(g_n[p][:, 0:4, :], ga, bc1(na_row[:, :], 4), ALU.mult), "gna")
                pool_n.done(tt(g_n[p][:, 4:8, :].rearrange("p h n -> p (h n)"), tk_in[p][:, 4 * BANK:], nb_row[:, :], ALU.mult), "gnb")

            def o_state_read(t, m, p):
                job_copied(pool, r_jobs, O_ST, t - 1)
                pool_o.done(tt(s_ad[:, :, :], s_a[:, :, :], bc(gt(G_EGL, t), HD), ALU.mult), "sad")

            def o_turn(t, m, p):
                wait(pool, bank_full[r_jobs.banks[O_TQ]], r_jobs.before(O_TQ, t) + 1)
                pool_o.done(tt(k_dk[:, :, :], qk_r[p][:, 4:8, :], bc(const("kdec"), HD), ALU.mult), "kdk")
                job_copied(pool, r_jobs, O_SR, t - 1)
                pool_o.done(tt(s_bd[:, :, :], s_b[:, :, :], bc(const("gend"), HD), ALU.mult), "sbd")

            def o_end(t, m, p):
                dve_o.wait(pool, "sumo", t)
                pool_o.done(pool.tensor_scalar(ms_o, ss_o, 1.0 / HD, EPS, ALU.mult, ALU.add), "ms")
                pool_o.wait(pool, "ms", t)
                pool_o.done(tt(rs_o, ms_o, neghalf[:, 0:8], ALU.pow), "rs")
                dve_o.wait(pool, "mixed", t)
                pool.dma_start(mixed_d[bass.ds(t * P, P), :], mixed[p][:, :, :].rearrange("p h n -> p (h n)")).then_inc(s_mst[p], 16)
            pool.memset(s_a[:, :, :], 0.0).then_inc(s_zero, 1)
            pool.memset(s_b[:, :, :], 0.0).then_inc(s_zero, 1)
            wait(pool, s_zero, 2)
            wait(pool, s_din, 80)
            wait(pool, s_gdve, 10)
            pieces = dict(ahead=ahead, n_norm=n_norm, n_turn=n_turn, n_scores=n_scores, n_first=n_first,
                          o_state_read=o_state_read, o_turn=o_turn, o_end=o_end, n_level6=n_gates)
            for s in range(1, LEV - 1):
                pieces[f"n_level{s}"] = level(s)
            d_steps(pool, pieces)
            for p in range(2):
                wait(pool, s_mst[p], 16 * T // 2)


        NL = GROUPS + EXPERTS
        o = base0 + 32 * KB + KD * NL * 4
        logits = sb("logits", [P, T, NL], o); o += T * NL * 4
        mix_in = [sb(f"mix_in{p}", [P, D], o + 4 * KB * p) for p in range(2)]; o += 8 * KB
        res2 = [sb(f"res2_{p}", [P, D], o + 4 * KB * p) for p in range(2)]; o += 8 * KB
        hn = [sb(f"hn{p}", [P, D], o + 4 * KB * p) for p in range(2)]; o += 8 * KB
        mix_t = sb("mix_t", [P, KD, P], o); o += 4 * KB
        hn_t = sb("hn_t", [P, KD, P], o); o += 4 * KB
        junk_e = sb("junk_e", [P, D], o); o += 4 * KB
        x4_d = dram("x4_d", (S, D))
        hn_d = dram("hn_d", (S, D))
        e_jobs = Jobs(base, [0, 1, 2, 3], T)
        eo_jobs = Jobs(base, [4, 5, 6], T)
        s_mixin = [sem(f"mix_in_in{p}") for p in range(2)]
        s_res2 = [sem(f"res2_in{p}") for p in range(2)]
        dve_e = Count("e_dve", "x4a x4b")
        act_e = Count("e_act", "sq hn")
        pool_e = Count("e_pool", "ms rs")
        s_x4st = [sem(f"x4_stored{p}") for p in range(2)]
        s_hnst = [sem(f"hn_stored{p}") for p in range(2)]
        ssE = stats[:, 90:91]; msE = stats[:, 91:92]; rsE = stats[:, 92:93]

        def e_sp(sp):
            for p in range(2):
                wait(sp, s_mst[p], 16 * T // 2)
            wait(sp, s_phase, PH_D)

            def step(new, old):
                if new:
                    t, m, p = new
                    if not isinstance(t, int) or t >= 2:
                        wait(sp, bank_full[1], e_jobs.before(1, t) - 1)
                        wait(sp, s_x4st[p], 16 * m)
                        act_e.wait(sp, "hn", t - 2)
                    sp.dma_start(mix_in[p][:, :], mixed_d[bass.ds(t * P, P), :]).then_inc(s_mixin[p], 16)
                    sp.dma_start(res2[p][:, :], x1_d[bass.ds(t * P, P), :]).then_inc(s_res2[p], 16)
            two_stage_from1(sp, step)

        def two_stage_from1(eng, step, tiles=T):
            step((0, 0, 0), None)
            step((1, 0, 1), (0, 0, 0))
            with eng.Fori(0, (tiles - 2) // 2) as i:
                step((2 * i + 2, i + 1, 0), (2 * i + 1, i, 1))
                step((2 * i + 3, i + 1, 1), (2 * i + 2, i + 1, 0))
            step(None, (tiles - 1, tiles // 2 - 1, 1))

        def e_pe(pe):
            def step(new, old):
                if new:
                    t, m, p = new
                    pe.wait_ge(s_mixin[p], 16 * m + 16)
                    for j in range(2):
                        b = job_start(pe, e_jobs, j, t)
                        for k in range(4):
                            mm = pe.transpose(b[:, k * P:(k + 1) * P], mix_in[p][:, (4 * j + k) * P:(4 * j + k + 1) * P], ident)
                        job_end(mm, e_jobs, j)
                if old:
                    t, m, p = old
                    act_e.wait(pe, "hn", t)
                    for j in range(2):
                        b = job_start(pe, eo_jobs, j, t)
                        for k in range(4):
                            mm = pe.transpose(b[:, k * P:(k + 1) * P], hn[p][:, (4 * j + k) * P:(4 * j + k + 1) * P], ident)
                        job_end(mm, eo_jobs, j)
                if new:
                    t, m, p = new
                    if isinstance(t, int) and t == 0:
                        pe.wait_ge(s_wo2, 16)
                    for j in range(2):
                        job_copied(pe, e_jobs, j, t)
                    for j in range(2):
                        b = job_start(pe, e_jobs, 2 + j, t)
                        for k in range(KD):
                            mm = pe.matmul(b, mix_t[:, k, :], w_o2[:, k, j * BANK:(j + 1) * BANK], start=(k == 0), stop=(k == KD - 1))
                        job_end(mm, e_jobs, 2 + j)
                if old:
                    t, m, p = old
                    if isinstance(t, int) and t == 0:
                        pe.wait_ge(s_wr, 32)
                    for j in range(2):
                        job_copied(pe, eo_jobs, j, t)
                    b = job_start(pe, eo_jobs, 2, t)
                    for k in range(KD):
                        mm = pe.matmul(b[:, 0:NL], hn_t[:, k, :], w_r[:, k, :], start=(k == 0), stop=(k == KD - 1))
                    job_end(mm, eo_jobs, 2)
            two_stage_from1(pe, step)

        def e_act(act):
            act.wait_ge(s_phase, PH_D)

            def step(new, old):
                if new:
                    t, m, p = new
                    b = job_read(act, e_jobs, 0, t)
                    job_done(act.activation(mix_t[:, 0:4, :].rearrange("p k n -> p (k n)"), b, ACT.Copy), e_jobs, 0)
                if new:
                    t, m, p = new
                    dve_e.wait(act, "x4b", t)
                    act_e.done(act.activation(junk_e[:, :], res2[p][:, :], ACT.Square, accum_out=ssE), "sq")
                    pool_e.wait(act, "rs", t)
                    wait(act, s_hnst[p], 16 * m)
                    act_e.done(act.activation(hn[p][:, :], res2[p][:, :], ACT.Copy, scale=rsE), "hn")
            two_stage_from1(act, step)

        def e_dve(v):
            v.wait_ge(s_phase, PH_D)

            def step(new, old):
                if new:
                    t, m, p = new
                    b = job_read(v, e_jobs, 1, t)
                    job_done(v.tensor_copy(mix_t[:, 4:8, :].rearrange("p k n -> p (k n)"), b), e_jobs, 1)
                if old:
                    t, m, p = old
                    for j in range(2):
                        b = job_read(v, eo_jobs, j, t)
                        ins = v.tensor_tensor(hn_t[:, 4 * j:4 * j + 4, :], b.rearrange("p (k n) -> p k n", k=4),
                                              bc(gain("ffn_norm")[:, 4 * j:4 * j + 4], P), ALU.mult)
                        job_done(ins, eo_jobs, j)
                if new:
                    t, m, p = new
                    v.wait_ge(s_res2[p], 16 * m + 16)
                    for j, name in enumerate(("x4a", "x4b")):
                        b = job_read(v, e_jobs, 2 + j, t)
                        half = res2[p][:, j * BANK:(j + 1) * BANK]
                        dve_e.done(v.tensor_tensor(half, b, half, ALU.add), name)
                        dve_e.wait(v, name, t)
                        v.sem_inc(bank_free[e_jobs.banks[2 + j]], 1)
                if old:
                    t, m, p = old
                    b = job_read(v, eo_jobs, 2, t)
                    job_done(v.tensor_copy(logits[:, bass.ds(t, 1), :].rearrange("p a n -> p (a n)"), b[:, 0:NL]), eo_jobs, 2)
            two_stage_from1(v, step)

        def e_pool(pool):
            for b, j in ((4, O_IN), (5, O_CR), (6, O_SR), (7, O_SB)):
                wait(pool, bank_free[b], r_jobs.before(j, T - 1) + 1)
            for b in range(4):
                wait(pool, bank_free[b], n_jobs.base[b] + n_jobs.banks.count(b) * T)
            pool.sem_inc(s_phase, 1)

            def step(new, old):
                if new:
                    t, m, p = new
                    act_e.wait(pool, "sq", t)
                    pool_e.done(pool.tensor_scalar(msE, ssE, 1.0 / D, EPS, ALU.mult, ALU.add), "ms")
                    pool_e.wait(pool, "ms", t)
                    pool_e.done(pool.tensor_tensor(rsE, msE, neghalf[:, 0:1], ALU.pow), "rs")
                    pool.dma_start(x4_d[bass.ds(t * P, P), :], res2[p][:, :]).then_inc(s_x4st[p], 16)
                    act_e.wait(pool, "hn", t)
                    pool.dma_start(hn_d[bass.ds(t * P, P), :], hn[p][:, :]).then_inc(s_hnst[p], 16)
            two_stage_from1(pool, step)
            for p in range(2):
                wait(pool, s_x4st[p], 16 * T // 2)
                wait(pool, s_hnst[p], 16 * T // 2)

        NBK = N_BLOCKS + 4
        oR = o
        E64 = EXPERTS

        def rt(name, shape, dt=F32):
            nonlocal o
            n = int(np.prod(shape[1:])) * 4
            r = sb(name, shape, o, dt)
            o += (n + 31) // 32 * 32
            return r

        r_g = rt("r_g", [P, T, GROUPS]); r_gd = rt("r_gd", [P, T, GROUPS]); r_ge = rt("r_ge", [P, T, GROUPS])
        r_oh = rt("r_oh", [P, T, GROUPS]); r_c = rt("r_c", [P, T, GROUPS])
        r_prod = rt("r_prod", [P, T, GROUPS, PER_GROUP]); r_es = rt("r_es", [P, T, PER_GROUP])
        r_e2 = rt("r_e2", [P, T, PER_GROUP])
        r_v = rt("r_v", [P, 24, T])
        oh = [rt(f"oh{k}", [P, T, E64]) for k in range(2)]
        r_m = rt("r_m", [P, T, E64]); r_cum = rt("r_cum", [P, T, E64]); r_carry = rt("r_carry", [P, T + 1, E64])
        r_pick = rt("r_pick", [P, T, E64])
        nblk = rt("nblk", [P, E64]); nblk_t = rt("nblk_t", [E64, P]); bstart = rt("bstart", [P, E64]); bend = rt("bend", [P, E64])
        r_rank = rt("r_rank", [P, 2 * T]); r_b0 = rt("r_b0", [P, 2 * T]); r_rb = rt("r_rb", [P, 2 * T])
        r_slot = rt("r_slot", [P, 2 * T]); r_blk = rt("r_blk", [P, 2 * T])
        ohs = [rt(f"ohs{q}", [P, P]) for q in range(2)]; ohb = [rt(f"ohb{q}", [P, NBK]) for q in range(2)]
        r_tab = rt("r_tab", [P, NBK]); r_eb = rt("r_eb", [P, 2]); r_cmp = rt("r_cmp", [P, E64])
        assert base_off + o <= 229344, o
        route_end = o
        o2 = base0
        w_tok = sb("w_tok", [P, 2, T], o2); o2 += 64
        asg_i = sb("asg_i", [P, NBK], o2, I32); o2 += 512
        src_i = sb("src_i", [P, NBK], o2, I32); o2 += 512
        eb_i = sb("eb_i", [P, 1], o2, I32); o2 += 32
        eb_row = sb("eb_row", [1, P], o2, I32); o2 += 512
        last_i = sb("last_i", [1, 1], o2, I32); o2 += 32
        base_m = base0 + 2 * KB
        assert o2 <= base_m
        eb_d = dram("eb_d", (P, 1), I32)
        rt_jobs = Jobs(base, [0, 1, 2, 3, 4], 1)
        s_rd = sem("route_dve"); s_ra = sem("route_act"); s_ohs = sem("slot_rows_ready"); s_ohp = sem("slot_rows_used")
        s_tab = sem("tables_ready"); s_eb = sem("block_experts_stored")
        VR = {n: i for i, n in enumerate("gmax gsum gidx m1 i1 m2 i2 ex den w0 e0 e1".split())}

        def r_dve(v):
            n = 0

            def link(ins):
                nonlocal n
                n += 1
                ins.then_inc(s_rd, 1)
                v.wait_ge(s_rd, n)
            vr = lambda name: r_v[:, VR[name], :]
            iota8 = const("iota")[:, 0:GROUPS]
            iota64 = const("iota")[:, 0:E64]
            tt, ts, stt = v.tensor_tensor, v.tensor_scalar, v.scalar_tensor_tensor

            def first(dst, flags, tmp):
                link(stt(tmp, flags, -1000.0, bc1(iota8, T), ALU.mult, ALU.add))
                link(v.tensor_reduce(dst, tmp, AX.X, ALU.min))
                link(ts(dst, dst, 1000.0, None, ALU.add))

            gl, el = logits[:, :, 0:GROUPS], logits[:, :, GROUPS:]
            for b in (6,):
                v.wait_ge(bank_free[b], eo_jobs.base[b] + T)
            link(v.tensor_reduce(vr("gmax"), gl, AX.X, ALU.max))
            link(tt(r_gd[:, :, :], gl, bc(vr("gmax"), GROUPS), ALU.subtract))
            link(ts(r_c[:, :, :], r_gd[:, :, :], 0.0, None, ALU.is_ge))
            first(vr("gidx"), r_c[:, :, :], r_g[:, :, :])
            link(tt(r_oh[:, :, :], bc1(iota8, T), bc(vr("gidx"), GROUPS), ALU.is_equal))
            link(tt(r_prod[:, :, :, :], el.rearrange("p t (g e) -> p t g e", g=GROUPS),
                    r_oh[:, :, :].unsqueeze(3).to_broadcast([P, T, GROUPS, PER_GROUP]), ALU.mult))
            link(v.tensor_reduce(r_es[:, :, :], r_prod[:, :, :, :].rearrange("p t g e -> p t e g"), AX.X, ALU.add))
            link(v.tensor_reduce(vr("m1"), r_es[:, :, :], AX.X, ALU.max))
            link(tt(r_es[:, :, :], r_es[:, :, :], bc(vr("m1"), PER_GROUP), ALU.subtract))
            link(ts(r_c[:, :, :], r_es[:, :, :], 0.0, None, ALU.is_ge))
            first(vr("i1"), r_c[:, :, :], r_g[:, :, :])
            link(tt(r_c[:, :, :], bc1(iota8, T), bc(vr("i1"), GROUPS), ALU.is_equal))
            link(stt(r_e2[:, :, :], r_c[:, :, :], -1.0e30, r_es[:, :, :], ALU.mult, ALU.add))
            link(v.tensor_reduce(vr("m2"), r_e2[:, :, :], AX.X, ALU.max))
            v.tensor_copy(vr("ex"), vr("m2")).then_inc(s_ra, 1)
            link(tt(r_c[:, :, :], r_e2[:, :, :], bc(vr("m2"), PER_GROUP), ALU.is_ge))
            first(vr("i2"), r_c[:, :, :], r_g[:, :, :])
            link(stt(vr("e0"), vr("gidx"), float(PER_GROUP), vr("i1"), ALU.mult, ALU.add))
            link(stt(vr("e1"), vr("gidx"), float(PER_GROUP), vr("i2"), ALU.mult, ALU.add))
            for k in range(2):
                link(tt(oh[k][:, :, :], bc1(iota64, T), bc(vr(f"e{k}"), E64), ALU.is_equal))
            tt(r_m[:, :, :], oh[0][:, :, :], oh[1][:, :, :], ALU.add).then_inc(s_tab, 1)
            v.wait_ge(s_ra, 3)
            link(v.tensor_reduce(vr("gsum"), r_ge[:, :, :], AX.X, ALU.add))
            link(ts(vr("den"), vr("ex"), 1.0, None, ALU.add))
            link(tt(vr("den"), vr("den"), vr("gsum"), ALU.mult))
            link(v.reciprocal(w_tok[:, 0, :], vr("den")))
            link(tt(w_tok[:, 1, :], w_tok[:, 0, :], vr("ex"), ALU.mult))
            link(v.memset(r_carry[:, 0, :], 0.0))
            b = job_read(v, rt_jobs, 1, 0)
            for t in range(T):
                link(tt(r_carry[:, t + 1, :], r_carry[:, t, :], b[:, t * E64:(t + 1) * E64], ALU.add))
            job_done(v.memset(r_rb[:, :], 0.0), rt_jobs, 1)
            link(v.memset(nblk[:, :], 0.0))
            for i in range(S // P):
                link(stt(nblk[:, :], r_carry[:, T, :], float(P * i), nblk[:, :], ALU.is_gt, ALU.add))
            v.tensor_copy(r_pick[:, 0, :], nblk[:, :]).then_inc(s_tab, 1)
            b = job_read(v, rt_jobs, 0, 0)
            job_done(tt(r_cum[:, :, :].rearrange("p t e -> p (t e)"), b, r_carry[:, 0:T, :].rearrange("p t e -> p (t e)"), ALU.add), rt_jobs, 0)
            b = job_read(v, rt_jobs, 2, 0)
            job_done(v.tensor_copy(nblk_t[:, :], b[0:E64, 0:P]), rt_jobs, 2)
            job_copied(v, rt_jobs, 0, 0)
            for k in range(2):
                link(tt(r_pick[:, :, :], oh[k][:, :, :], r_cum[:, :, :], ALU.mult))
                link(v.tensor_reduce(r_rank[:, k * T:(k + 1) * T], r_pick[:, :, :], AX.X, ALU.add))
            for i in range(1, S // P):
                link(stt(r_rb[:, :], r_rank[:, :], float(P * i), r_rb[:, :], ALU.is_ge, ALU.add))
            b = job_read(v, rt_jobs, 3, 0)
            job_done(v.tensor_copy(bstart[:, :], b[:, 0:E64]), rt_jobs, 3)
            job_copied(v, rt_jobs, 3, 0)
            for k in range(2):
                link(tt(r_pick[:, :, :], oh[k][:, :, :], bc1(bstart[:, :], T), ALU.mult))
                link(v.tensor_reduce(r_b0[:, k * T:(k + 1) * T], r_pick[:, :, :], AX.X, ALU.add))
            link(stt(r_slot[:, :], r_rb[:, :], -float(P), r_rank[:, :], ALU.mult, ALU.add))
            link(tt(r_blk[:, :], r_b0[:, :], r_rb[:, :], ALU.add))
            for a in range(2 * T):
                k, t = a // T, a % T
                q = a % 2
                wait(v, s_ohp, a - 1)
                v.tensor_scalar(ohs[q][:, :], const("iota"), r_slot[:, a:a + 1], None, ALU.is_equal).then_inc(s_ohs, 1)
                v.tensor_scalar(ohb[q][:, :], const("iota")[:, 0:NBK], r_blk[:, a:a + 1], const("asg")[:, a:a + 1],
                                ALU.is_equal, ALU.mult).then_inc(s_ohs, 1)
            link(tt(bend[:, :], bstart[:, :], nblk[:, :], ALU.add))
            link(ts(r_cmp[:, :], bend[:, :], const("pcol"), None, ALU.is_le))
            link(v.tensor_reduce(r_eb[:, 0:1], r_cmp[:, :], AX.X, ALU.add))
            link(ts(r_eb[:, 0:1], r_eb[:, 0:1], float(EXPERTS - 1), None, ALU.min))
            link(ts(last_i[0:1, :], bend[0:1, E64 - 1:E64], -1.0, None, ALU.add))
            v.tensor_copy(eb_i[:, :], r_eb[:, 0:1]).then_inc(s_tab, 1)
            b = job_read(v, rt_jobs, 4, 0)
            link(ts(asg_i[:, :], b[:, 0:NBK], NOWHERE, None, ALU.add))
            job_done(ts(r_tab[:, :], b[:, 0:NBK], NOWHERE, None, ALU.add), rt_jobs, 4)
            v.tensor_scalar(src_i[:, :], asg_i[:, :], 1, None, ALU.logical_shift_right).then_inc(s_tab, 1)

        def r_act(act):
            act.wait_ge(s_rd, 2)
            act.activation(r_ge[:, :, :], r_gd[:, :, :], ACT.Exp).then_inc(s_ra2, 1)
            act.wait_ge(s_ra, 1)
            act.activation(r_v[:, VR["ex"], :], r_v[:, VR["ex"], :], ACT.Exp).then_inc(s_ra2, 1)
            act.wait_ge(s_ra2, 2)
            act.sem_inc(s_ra, 2)

        s_ra2 = sem("route_act_own")

        def r_pe(pe):
            pe.wait_ge(s_tab, 1)
            m_ = r_m[:, :, :].rearrange("p t e -> p (t e)")
            b = job_start(pe, rt_jobs, 0, 0)
            job_end(pe.matmul(b, const("before"), m_, start=True, stop=True), rt_jobs, 0)
            b = job_start(pe, rt_jobs, 1, 0)
            job_end(pe.matmul(b, ones, m_, start=True, stop=True), rt_jobs, 1)
            pe.wait_ge(s_tab, 2)
            b = job_start(pe, rt_jobs, 2, 0)
            job_end(pe.transpose(b[0:E64, 0:P], nblk[:, :], ident), rt_jobs, 2)
            job_copied(pe, rt_jobs, 2, 0)
            b = job_start(pe, rt_jobs, 3, 0)
            job_end(pe.matmul(b[:, 0:E64], nblk_t[:, :], const("before")[0:E64, 0:E64], start=True, stop=True), rt_jobs, 3)
            b = job_start(pe, rt_jobs, 4, 0)
            for a in range(2 * T):
                q = a % 2
                pe.wait_ge(s_ohs, 2 * a + 2)
                mm = pe.matmul(b[:, 0:NBK], ohs[q][:, :], ohb[q][:, :], start=(a == 0), stop=(a == 2 * T - 1))
                if a < 2 * T - 1:
                    mm.then_inc(s_ohp, 1)
            job_end(mm, rt_jobs, 4)

        o = base_m
        NB = 4
        w_gu = [sb(f"w_gu{q}", [P, KD, 2 * DE], o + 16 * KB * q) for q in range(NB)]; o += 16 * KB * NB
        w_d = [sb(f"w_d{q}", [P, 2, D], o + 8 * KB * q) for q in range(NB)]; o += 8 * KB * NB
        assert o >= route_end
        rows = [sb(f"rows{q}", [P, D], o + 4 * KB * q) for q in range(NB)]; o += 4 * KB * NB
        rows_t = sb("rows_t", [P, KD, P], o); o += 4 * KB
        act_g = sb("act_g", [P, DE], o); o += KB
        act_s = sb("act_s", [P, DE], o); o += KB
        act_tt = sb("act_tt", [P, 2, P], o); o += KB
        y_out = [sb(f"y_out{p}", [P, D], o + 4 * KB * p) for p in range(2)]; o += 8 * KB
        gidx = [sb(f"gidx{q}", [P, 1], o + 32 * q, I32) for q in range(NB)]; o += 32 * NB
        sidx = [sb(f"sidx{p}", [P, 1], o + 32 * p, I32) for p in range(2)]; o += 64
        assert base_off + o <= 229344, (o, base_off + o - 229344)
        y_d = dram("y_d", (2 * S, D))
        s_load = [sem(f"w_gu_in{q}") for q in range(NB)]
        s_loadd = [sem(f"w_d_in{q}") for q in range(NB)]
        s_gath = [sem(f"rows_in{q}") for q in range(NB)]
        s_sct = [sem(f"y_out_stored{p}") for p in range(2)]
        m_jobs = Jobs(base, [0, 1, 2, 3, 4, 5], 0)
        s_actg = sem("gate_silu"); s_acts = sem("act_ready"); s_gi = sem("index_copied"); s_si = sem("store_index_copied")

        def blocks(eng, first, body, last, start=1):
            eng.wait_ge(s_tab, 4)
            end = eng.value_load(last_i[0:1, 0:1], min_val=2 * S // P - 1, max_val=N_BLOCKS - 1)
            first()
            with eng.Fori(0, (N_BLOCKS - start + NB - 1) // NB) as i:
                for j in range(NB):
                    b = NB * i + (start + j)
                    with eng.If(b <= end):
                        body(b, i, j)
            last(end)

        def moe_sp(sp):
            wait(sp, s_tab, 4)
            for p in range(2):
                wait(sp, s_x4st[p], 16 * T // 2)
                wait(sp, s_hnst[p], 16 * T // 2)
            sp.dma_start(eb_d, eb_i[:, :]).then_inc(s_eb, 16)
            wait(sp, s_eb, 16)
            sp.dma_start(eb_row[0:1, :], eb_d.rearrange("p a -> a p")).then_inc(s_eb, 16)
            wait(sp, s_eb, 32)

            def load_gu(b, p):
                e = sp.value_load(eb_row[0:1, bass.ds(b, 1)], min_val=0, max_val=EXPERTS - 1)
                for w, c in (("w_gate_2", 0), ("w_up_2", DE)):
                    src = A[w][0].rearrange("e (k p) n -> e p k n", p=P)[bass.ds(e, 1), :, :, :].rearrange("e p k n -> (e p) k n")
                    sp.dma_start(w_gu[p][:, :, c:c + DE], src).then_inc(s_load[p], 16)

            def load_d(b, p):
                e = sp.value_load(eb_row[0:1, bass.ds(b, 1)], min_val=0, max_val=EXPERTS - 1)
                src = A["w_down_2"][0].rearrange("e (k p) n -> e p k n", p=P)[bass.ds(e, 1), :, :, :].rearrange("e p k n -> (e p) k n")
                sp.dma_start(w_d[p][:, :, :], src).then_inc(s_loadd[p], 16)

            def first():
                for b in range(NB):
                    load_gu(b, b)
                    load_d(b, b)

            def body(b, i, j):
                wait(sp, bank_full[2], m_jobs.base[2] + b - (NB - 1))
                load_gu(b, j)
                wait(sp, bank_full[5], m_jobs.base[5] + b - (NB - 1))
                load_d(b, j)
            blocks(sp, first, body, lambda end: None, start=NB)

        def moe_pe(pe):
            bf = lambda b_: bank_free[b_]

            def turn(b, p):
                for j in range(2):
                    pe.wait_ge(bf(j), m_jobs.base[j] + b)
                    for k in range(4):
                        mm = pe.transpose(ps[:, j, k * P:(k + 1) * P], rows[p][:, (4 * j + k) * P:(4 * j + k + 1) * P], ident)
                    mm.then_inc(bank_full[j], 1)

            def gate_up(b, m, p):
                for j in range(2):
                    pe.wait_ge(bf(j), m_jobs.base[j] + b + 1)
                pe.wait_ge(s_load[p], 32 * m + 32)
                pe.wait_ge(bf(2), m_jobs.base[2] + b)
                for k in range(KD):
                    mm = pe.matmul(ps[:, 2, :], rows_t[:, k, :], w_gu[p][:, k, :], start=(k == 0), stop=(k == KD - 1))
                mm.then_inc(bank_full[2], 1)

            def turn_act(b):
                pe.wait_ge(s_acts, b + 1)
                pe.wait_ge(bf(3), m_jobs.base[3] + b)
                for k in range(2):
                    mm = pe.transpose(ps[:, 3, k * P:(k + 1) * P], act_s[:, k * P:(k + 1) * P], ident)
                mm.then_inc(bank_full[3], 1)

            def down(b, wd):
                pe.wait_ge(bf(3), m_jobs.base[3] + b + 1)
                for j in range(2):
                    pe.wait_ge(bf(4 + j), m_jobs.base[4 + j] + b)
                    for k in range(2):
                        mm = pe.matmul(ps[:, 4 + j, :], act_tt[:, k, :], wd[:, k, j * BANK:(j + 1) * BANK], start=(k == 0), stop=(k == 1))
                    mm.then_inc(bank_full[4 + j], 1)

            def first():
                pe.wait_ge(s_gath[0], 16)
                turn(0, 0)
                gate_up(0, 0, 0)
                pe.wait_ge(s_gath[1], 16)
                turn(1, 1)
                turn_act(0)

            def body(b, i, j):
                gate_up(b, i + (1 + j) // NB, (1 + j) % NB)
                q = (2 + j) % NB
                pe.wait_ge(s_gath[q], 16 * (i + ((2 + j) // NB + 1)))
                turn(b + 1, q)
                pe.wait_ge(s_loadd[j], 16 * (i + 1))
                down(b - 1, w_d[j])
                turn_act(b)

            def last(end):
                for q in range(NB):
                    with pe.If(end % NB == q):
                        pe.wait_ge(s_loadd[q], 16 * (end // NB) + 16)
                        down(end, w_d[q])
            blocks(pe, first, body, last)

        def moe_act(act):
            def half_rows(b):
                act.wait_ge(bank_full[0], m_jobs.base[0] + b + 1)
                for k in range(4):
                    ins = act.activation(rows_t[:, k, :], ps[:, 0, k * P:(k + 1) * P], ACT.Copy, scale=gain("ffn_norm")[:, k:k + 1])
                ins.then_inc(bank_free[0], 1)

            def silu(b):
                act.wait_ge(bank_full[2], m_jobs.base[2] + b + 1)
                act.activation(act_g[:, :], ps[:, 2, 0:DE], ACT.Silu).then_inc(s_actg, 1)

            def turned(b):
                act.wait_ge(bank_full[3], m_jobs.base[3] + b + 1)
                act.activation(act_tt[:, :, :].rearrange("p k n -> p (k n)"), ps[:, 3, 0:DE], ACT.Copy).then_inc(bank_free[3], 1)

            def y_half(b, mult, p):
                act.wait_ge(bank_full[4], m_jobs.base[4] + b + 1)
                wait(act, s_sct[p], mult)
                act.activation(y_out[p][:, 0:BANK], ps[:, 4, :], ACT.Copy).then_inc(bank_free[4], 1)

            def first():
                half_rows(0)
                silu(0)
                half_rows(1)
                turned(0)

            def body(b, i, j):
                silu(b)
                half_rows(b + 1)
                y_half(b - 1, 16 * (2 * i + j // 2), j % 2)
                turned(b)

            def last(end):
                for p in range(2):
                    with act.If(end % 2 == p):
                        y_half(end, 16 * (end // 2), p)
            blocks(act, first, body, last)

        def moe_dve(v):
            def half_rows(b):
                v.wait_ge(bank_full[1], m_jobs.base[1] + b + 1)
                v.tensor_tensor(rows_t[:, 4:8, :], ps[:, 1, :].rearrange("p (k n) -> p k n", k=4),
                                bc(gain("ffn_norm")[:, 4:8], P), ALU.mult).then_inc(bank_free[1], 1)

            def product(b):
                v.wait_ge(s_actg, b + 1)
                v.tensor_tensor(act_s[:, :], act_g[:, :], ps[:, 2, DE:], ALU.mult).then_inc(s_acts, 1)
                v.wait_ge(s_acts, b + 1)
                v.sem_inc(bank_free[2], 1)

            def y_half(b, mult, p):
                v.wait_ge(bank_full[5], m_jobs.base[5] + b + 1)
                wait(v, s_sct[p], mult)
                v.tensor_copy(y_out[p][:, BANK:], ps[:, 5, :]).then_inc(bank_free[5], 1)

            def first():
                half_rows(0)
                product(0)
                half_rows(1)

            def body(b, i, j):
                product(b)
                half_rows(b + 1)
                y_half(b - 1, 16 * (2 * i + j // 2), j % 2)

            def last(end):
                for p in range(2):
                    with v.If(end % 2 == p):
                        y_half(end, 16 * (end // 2), p)
            blocks(v, first, body, last)

        def moe_pool(pool):
            def gather(b, p):
                pool.tensor_copy(gidx[p][:, :], src_i[:, bass.ds(b, 1)]).then_inc(s_gi, 1)
                wait(pool, s_gi, b + (NB + 1))
                pool.indirect_dma_start(out=rows[p][:, :], out_offset=None, in_=hn_d,
                                        in_offset=bass.IndirectOffsetOnAxis(ap=gidx[p][:, 0:1], axis=0),
                                        bounds_check=S - 1, oob_is_err=False).then_inc(s_gath[p], 16)

            def scatter(b, p):
                pool.tensor_copy(sidx[p][:, :], asg_i[:, bass.ds(b, 1)]).then_inc(s_si, 1)
                wait(pool, s_si, b + 1)
                for j in (4, 5):
                    wait(pool, bank_free[j], m_jobs.base[j] + b + 1)
                pool.indirect_dma_start(out=y_d, out_offset=bass.IndirectOffsetOnAxis(ap=sidx[p][:, 0:1], axis=0),
                                        in_=y_out[p][:, :], in_offset=None,
                                        bounds_check=2 * S - 1, oob_is_err=False).then_inc(s_sct[p], 16)

            def first():
                wait(pool, s_gi, NB)
                for b in range(3):
                    gather(b, b)

            def body(b, i, j):
                wait(pool, bank_full[1], m_jobs.base[1] + b - 1)
                gather(b + 2, (3 + j) % NB)
                wait(pool, s_sct[j % 2], 16 * (2 * i + j // 2))
                scatter(b - 1, j % 2)

            def last(end):
                for p in range(2):
                    with pool.If(end % 2 == p):
                        wait(pool, s_sct[p], 16 * (end // 2))
                        scatter(end, p)
                wait(pool, s_sct[0], 16 * ((end + 2) // 2))
                wait(pool, s_sct[1], 16 * ((end + 1) // 2))
                for q in range(NB):
                    wait(pool, s_gath[q], 16 * ((end + (NB + 2 - q)) // NB))
                pool.sem_inc(s_phase, 1)
            for q in range(NB):
                pool.memset(rows[q][:, :], 0.0).then_inc(s_gi, 1)
            blocks(pool, first, body, last)


        o = base_m
        xf = [sb(f"xf{p}", [P, D], o + 4 * KB * p) for p in range(2)]; o += 8 * KB
        yf = [sb(f"yf{p}", [P, 2, D], o + 8 * KB * p) for p in range(2)]; o += 16 * KB
        outf = [sb(f"outf{p}", [P, D], o + 4 * KB * p) for p in range(2)]; o += 8 * KB
        fn2 = sb("fn2", [P, D], o); o += 4 * KB
        junk_f = sb("junk_f", [P, D], o); o += 4 * KB
        s_xf = [sem(f"xf_in{p}") for p in range(2)]
        s_yf = [sem(f"yf_in{p}") for p in range(2)]
        s_fn2 = sem("fn2_in")
        dve_f = Count("f_dve", "y0 y1 out", after=dve_e)
        act_f = Count("f_act", "sq", after=act_e)
        pool_f = Count("f_pool", "ms rs", after=pool_e)
        s_out = [sem(f"out_stored{p}") for p in range(2)]
        ssF = stats[:, 94:95]; msF = stats[:, 95:96]; rsF = stats[:, 96:97]

        def f_sp(sp):
            wait(sp, s_phase, PH_M)
            sp.dma_start(fn2[:, :], A["final_norm_2"].partition_broadcast(P)).then_inc(s_fn2, 16)

            def load(t, p):
                sp.dma_start(xf[p][:, :], x4_d[bass.ds(t * P, P), :]).then_inc(s_xf[p], 16)
                sp.dma_start(yf[p][:, :, :], y_d[bass.ds(t * 2 * P, 2 * P), :].rearrange("(p k) n -> p k n", k=2)).then_inc(s_yf[p], 16)
            load(0, 0)
            load(1, 1)

            def store(t, p):
                dve_f.wait(sp, "out", t)
                sp.dma_start(out[0, bass.ds(t * P, P), :], outf[p][:, :]).then_inc(s_out[p], 16)
            with sp.Fori(0, T // 2 - 1) as i:
                for p in range(2):
                    store(2 * i + p, p)
                    load(2 * i + p + 2, p)
            for p in range(2):
                store(T - 2 + p, p)
            for p in range(2):
                wait(sp, s_out[p], 16 * T // 2)

        def f_dve(v):
            v.wait_ge(s_fn2, 16)
            with v.Fori(0, T // 2) as i:
                for p in range(2):
                    t = 2 * i + p
                    v.wait_ge(s_xf[p], 16 * i + 16)
                    v.wait_ge(s_yf[p], 16 * i + 16)
                    for k in range(2):
                        dve_f.done(v.scalar_tensor_tensor(xf[p][:, :], yf[p][:, k, :], w_tok[:, k, bass.ds(t, 1)], xf[p][:, :],
                                                          ALU.mult, ALU.add), f"y{k}")
                        dve_f.wait(v, f"y{k}", t)
                    pool_f.wait(v, "rs", t)
                    v.wait_ge(s_out[p], 16 * i)
                    dve_f.done(v.scalar_tensor_tensor(outf[p][:, :], xf[p][:, :], rsF, fn2[:, :], ALU.mult, ALU.mult), "out")

        def f_act(act):
            with act.Fori(0, T // 2) as i:
                for p in range(2):
                    t = 2 * i + p
                    dve_f.wait(act, "y1", t)
                    act_f.done(act.activation(junk_f[:, :], xf[p][:, :], ACT.Square, accum_out=ssF), "sq")

        def f_pool(pool):
            with pool.Fori(0, T // 2) as i:
                for p in range(2):
                    t = 2 * i + p
                    act_f.wait(pool, "sq", t)
                    pool_f.done(pool.tensor_scalar(msF, ssF, 1.0 / D, EPS, ALU.mult, ALU.add), "ms")
                    pool_f.wait(pool, "ms", t)
                    pool_f.done(pool.tensor_tensor(rsF, msF, neghalf[:, 0:1], ALU.pow), "rs")

        block = ctx.enter_context(nc.Block())

        @block.sync
        def _(sp):
            setup_sp(sp)
            a_sp(sp)
            att_sp(sp)
            b_sp(sp)
            c_sp(sp)
            d0_sp(sp)
            e_sp(sp)
            moe_sp(sp)
            f_sp(sp)

        @block.tensor
        def _(pe):
            setup_pe(pe)
            a_pe(pe)
            att_pe(pe)
            b_pe(pe)
            c_pe(pe)
            d0_pe(pe)
            d_pe(pe)
            e_pe(pe)
            r_pe(pe)
            moe_pe(pe)

        @block.scalar
        def _(act):
            setup_act(act)
            a_act(act)
            att_act(act)
            b_act(act)
            c_act(act)
            d0_act(act)
            d_act(act)
            e_act(act)
            r_act(act)
            moe_act(act)
            f_act(act)

        @block.vector
        def _(v):
            setup_dve(v)
            a_dve(v)
            att_dve(v)
            b_dve(v)
            c_dve(v)
            d0_dve(v)
            d_dve(v)
            e_dve(v)
            r_dve(v)
            moe_dve(v)
            f_dve(v)

        @block.gpsimd
        def _(pool):
            a_pool(pool)
            phase_a_end(pool)
            b_pool(pool)
            b_end(pool)
            c_pool(pool)
            d_pool(pool)
            e_pool(pool)
            moe_pool(pool)
            f_pool(pool)


_INS = ["x", "p", "positions", "norm_g", "mla_w_in", "mla_q_norm", "mla_w_q_b", "mla_kv_norm", "mla_w_kv_b",
        "mla_w_out", "ple_proj", "ple_gate", "final_norm", "attn_norm_2", "w_in_2", "conv_a_2", "a_log_2", "dt_bias_2",
        "norm_a_2", "norm_b_2", "w_out_2", "ffn_norm_2", "w_router_group_2", "w_router_expert_2", "w_gate_2", "w_up_2",
        "w_down_2", "final_norm_2"]


def kernel(**inputs):
    import concourse.bacc as bacc
    from concourse.bass_utils import run_bass_kernel_spmd

    nc = bacc.Bacc("TRN2", target_bir_lowering=False, num_devices=1)
    arrays = {name: np.ascontiguousarray(inputs[name]) for name in _INS}
    arrays["c_table"], arrays["c_rot"] = constants()
    A = {name: nc.dram_tensor(name, a.shape, mybir.dt.from_np(a.dtype), kind="ExternalInput").ap()
         for name, a in arrays.items()}
    out = nc.dram_tensor("out", (1, S, D), F32, kind="ExternalOutput").ap()
    build(nc, A, out)
    r = run_bass_kernel_spmd(nc, [arrays], core_ids=[0])
    return r.results[0]["out"]
```
